# Optimizing a Trainium2 kernel written in Bass

```python
import jax, jax.numpy as jnp
from jax import lax
import numpy as np

D_MODEL = 1024
BATCH = 1
SEQ = 256
DEPTH = 2

CHUNK = 64
N_EVEN = (DEPTH + 1) // 2
N_ODD = DEPTH // 2
EPS = 1e-6

POOL_GROUPS = 4
POOL_CH = D_MODEL // 8
POOL_WIDTH = POOL_GROUPS * POOL_CH
POOL_WINDOWS = (2, 4, 8, 16)

MLA_HEADS = 8
MLA_NOPE = D_MODEL // 16
MLA_ROPE = D_MODEL // 32
MLA_V = D_MODEL // 16
MLA_Q_RANK = D_MODEL // 4
MLA_KV_RANK = D_MODEL // 8
ROPE_THETA = 10000.0
Q_BLOCK = 128
EVEN_IN = POOL_WIDTH + MLA_Q_RANK + MLA_KV_RANK + MLA_ROPE
EVEN_MIX = POOL_WIDTH + MLA_HEADS * MLA_V

CA_HEADS = 8
CA_HEAD_DIM = D_MODEL // 16
CA_LEFT_CHUNKS = 8
REL_CLIP = 128

SGU_GROUPS = 4
SGU_CH = D_MODEL // 8
SGU_WIDTH = SGU_GROUPS * SGU_CH
SGU_CHUNK = 128
ODD_IN = 3 * CA_HEADS * CA_HEAD_DIM + 2 * SGU_WIDTH
ODD_MIX = CA_HEADS * CA_HEAD_DIM + SGU_WIDTH

D_FF = 2816
N_EXPERTS = 8
TOP_K = 2
EXPERT_FF = 3584

kernel_name = 'hybrid_chunk_causal_pool_mla_relattn_sgu_moe'

def rms_norm(x, g):
    xf = x.astype(jnp.float32)
    y = xf * lax.rsqrt(jnp.mean(xf * xf, axis=-1, keepdims=True) + EPS)
    return (y * g.astype(jnp.float32)).astype(x.dtype)

def layer_norm(x, g, b):
    xf = x.astype(jnp.float32)
    mu = jnp.mean(xf, axis=-1, keepdims=True)
    xc = xf - mu
    y = xc * lax.rsqrt(jnp.mean(xc * xc, axis=-1, keepdims=True) + EPS)
    return (y * g.astype(jnp.float32) + b.astype(jnp.float32)).astype(x.dtype)

def swiglu(x, w_gate, w_up, w_down):
    return (jax.nn.silu(x @ w_gate) * (x @ w_up)) @ w_down

def rope_tables(s):
    inv = 1.0 / (ROPE_THETA ** (jnp.arange(0, MLA_ROPE, 2, dtype=jnp.float32) / MLA_ROPE))
    ang = jnp.arange(s, dtype=jnp.float32)[:, None] * inv[None, :]
    return jnp.cos(ang), jnp.sin(ang)

def apply_rope(x, cos, sin):
    x1, x2 = jnp.split(x, 2, axis=-1)
    return jnp.concatenate([x1 * cos - x2 * sin, x2 * cos + x1 * sin], axis=-1).astype(x.dtype)

def multiscale_pool(a, w_pool, scale):
    b, s, g, c = a.shape
    af = a.astype(jnp.float32)
    cs = jnp.concatenate([jnp.zeros((b, 1, g, c), jnp.float32), jnp.cumsum(af, axis=1)], axis=1)
    t = jnp.arange(s)[:, None]
    win = jnp.array(POOL_WINDOWS, dtype=jnp.int32)[None, :]
    lo = jnp.maximum(t + 1 - win, 0)
    lo_sum = cs[:, lo, jnp.arange(g)[None, :]]
    count = (t + 1 - lo).astype(jnp.float32)[None, :, :, None]
    pooled = ((cs[:, 1:] - lo_sum) / count - af).astype(a.dtype)
    y = jnp.einsum('bsgc,gcd->bsgd', pooled, w_pool) * scale
    return y.reshape(b, s, g * c)

def mla_attention(q, k, v):
    b, s, h, dq = q.shape
    nqb = s // Q_BLOCK
    scale = dq ** -0.5
    k_chunk = jnp.arange(s) // CHUNK
    q_blocks = q.reshape(b, nqb, Q_BLOCK, h, dq).transpose(1, 0, 2, 3, 4)

    def block(args):
        qb, start = args
        q_chunk = (start + jnp.arange(Q_BLOCK)) // CHUNK
        sc = jnp.einsum('bqhd,bkhd->bhqk', qb, k, preferred_element_type=jnp.float32) * scale
        sc = jnp.where(k_chunk[None, :] <= q_chunk[:, None], sc, -jnp.inf)
        p = jax.nn.softmax(sc, axis=-1).astype(v.dtype)
        return jnp.einsum('bhqk,bkhd->bqhd', p, v)

    out = lax.map(block, (q_blocks, jnp.arange(nqb) * Q_BLOCK))
    return out.transpose(1, 0, 2, 3, 4).reshape(b, s, h, v.shape[-1])

def chunk_band_attention(q, k, v, rel_bias):
    b, s, h, d = q.shape
    nc = s // CHUNK
    band = (CA_LEFT_CHUNKS + 1) * CHUNK
    qc = q.reshape(b, nc, CHUNK, h, d)

    def gather_band(t):
        tp = jnp.pad(t.reshape(b, nc, CHUNK, h, d), ((0, 0), (CA_LEFT_CHUNKS, 0), (0, 0), (0, 0), (0, 0)))
        return jnp.concatenate([tp[:, j:j + nc] for j in range(CA_LEFT_CHUNKS + 1)], axis=2)

    kb, vb = gather_band(k), gather_band(v)
    sc = jnp.einsum('bnqhd,bnkhd->bhnqk', qc, kb, preferred_element_type=jnp.float32) * (d ** -0.5)
    rel = jnp.arange(CHUNK)[:, None] + CA_LEFT_CHUNKS * CHUNK - jnp.arange(band)[None, :]
    bias = rel_bias[:, jnp.clip(rel, -REL_CLIP, REL_CLIP) + REL_CLIP].astype(jnp.float32)
    valid = (jnp.arange(nc)[:, None] - CA_LEFT_CHUNKS + jnp.arange(band)[None, :] // CHUNK) >= 0
    sc = jnp.where(valid[None, None, :, None, :], sc + bias[:, None], -jnp.inf)
    p = jax.nn.softmax(sc, axis=-1).astype(vb.dtype)
    out = jnp.einsum('bhnqk,bnkhd->bnqhd', p, vb)
    return out.reshape(b, s, h, d)

def spatial_gating(u, v, norm_g, norm_b, w_s, b_s):
    b, s, g, c = v.shape
    n = s // SGU_CHUNK
    vn = layer_norm(v, norm_g, norm_b).reshape(b, n, SGU_CHUNK, g, c)
    causal = jnp.tril(jnp.ones((SGU_CHUNK, SGU_CHUNK), dtype=bool))
    w = jnp.where(causal[None], w_s, jnp.zeros_like(w_s))
    mixed = jnp.einsum('gts,bnsgc->bntgc', w, vn) + b_s.T[None, None, :, :, None]
    return u * mixed.reshape(b, s, g, c)

def moe_swiglu(h, router, w_gate, w_up, w_down):
    b, s, d = h.shape
    t = h.reshape(b * s, d)
    logits = (t @ router).astype(jnp.float32)
    top_val, top_idx = lax.top_k(logits, TOP_K)
    top_w = jax.nn.softmax(top_val, axis=-1)
    gates = jnp.sum(jax.nn.one_hot(top_idx, N_EXPERTS, dtype=jnp.float32) * top_w[..., None], axis=1)
    out = jnp.zeros((b * s, d), jnp.float32)
    for e in range(N_EXPERTS):
        out = out + gates[:, e:e + 1] * swiglu(t, w_gate[e], w_up[e], w_down[e]).astype(jnp.float32)
    return out.astype(h.dtype).reshape(b, s, d)

def even_mixer(h, w_in, pool_w, pool_scale, q_norm, w_q_up, kv_norm, w_kv_up, w_out, cos, sin):
    b, s, _ = h.shape
    z = h @ w_in
    a, cq, ckv, kr = jnp.split(z, [POOL_WIDTH, POOL_WIDTH + MLA_Q_RANK, POOL_WIDTH + MLA_Q_RANK + MLA_KV_RANK], axis=-1)
    pool = multiscale_pool(a.reshape(b, s, POOL_GROUPS, POOL_CH), pool_w, pool_scale)
    q = (rms_norm(cq, q_norm) @ w_q_up).reshape(b, s, MLA_HEADS, MLA_NOPE + MLA_ROPE)
    q_nope, q_rope = jnp.split(q, [MLA_NOPE], axis=-1)
    kv = (rms_norm(ckv, kv_norm) @ w_kv_up).reshape(b, s, MLA_HEADS, MLA_NOPE + MLA_V)
    k_nope, v = jnp.split(kv, [MLA_NOPE], axis=-1)
    q_rope = apply_rope(q_rope, cos[None, :, None], sin[None, :, None])
    k_rope = apply_rope(kr, cos[None], sin[None])
    qf = jnp.concatenate([q_nope, q_rope], axis=-1)
    kf = jnp.concatenate([k_nope, jnp.broadcast_to(k_rope[:, :, None], (b, s, MLA_HEADS, MLA_ROPE))], axis=-1)
    att = mla_attention(qf, kf, v).reshape(b, s, MLA_HEADS * MLA_V)
    return jnp.concatenate([pool, att], axis=-1) @ w_out

def odd_mixer(h, w_in, rel_bias, sgu_norm_g, sgu_norm_b, sgu_w, sgu_b, w_out):
    b, s, _ = h.shape
    z = h @ w_in
    qkv, uv = jnp.split(z, [3 * CA_HEADS * CA_HEAD_DIM], axis=-1)
    q, k, v = [t.reshape(b, s, CA_HEADS, CA_HEAD_DIM) for t in jnp.split(qkv, 3, axis=-1)]
    att = chunk_band_attention(q, k, v, rel_bias).reshape(b, s, CA_HEADS * CA_HEAD_DIM)
    u, gv = jnp.split(jax.nn.gelu(uv), 2, axis=-1)
    sg = spatial_gating(u.reshape(b, s, SGU_GROUPS, SGU_CH), gv.reshape(b, s, SGU_GROUPS, SGU_CH),
                        sgu_norm_g, sgu_norm_b, sgu_w, sgu_b).reshape(b, s, SGU_WIDTH)
    return jnp.concatenate([att, sg], axis=-1) @ w_out

def setup_inputs(seed: int = 0) -> dict:
    key = jax.random.key(seed)
    ks = iter(jax.random.split(key, 32))
    nrm = lambda shape, scale: jax.random.normal(next(ks), shape, jnp.float32) * scale
    gain = lambda shape: 1.0 + nrm(shape, 0.1)
    E, O, D = N_EVEN, N_ODD, D_MODEL
    res = (2 * DEPTH) ** -0.5
    return {
        'x': nrm((BATCH, SEQ, D), 1.0),
        'ev_norm_mix': gain((E, D)),
        'ev_w_in': nrm((E, D, EVEN_IN), D ** -0.5),
        'ev_pool_w': nrm((E, POOL_GROUPS, POOL_CH, POOL_CH), POOL_CH ** -0.5),
        'ev_pool_scale': gain((E, POOL_GROUPS, POOL_CH)),
        'ev_q_norm': gain((E, MLA_Q_RANK)),
        'ev_w_q_up': nrm((E, MLA_Q_RANK, MLA_HEADS * (MLA_NOPE + MLA_ROPE)), MLA_Q_RANK ** -0.5),
        'ev_kv_norm': gain((E, MLA_KV_RANK)),
        'ev_w_kv_up': nrm((E, MLA_KV_RANK, MLA_HEADS * (MLA_NOPE + MLA_V)), MLA_KV_RANK ** -0.5),
        'ev_w_out': nrm((E, EVEN_MIX, D), EVEN_MIX ** -0.5 * res),
        'ev_norm_ffn': gain((E, D)),
        'ev_ffn_w_gate': nrm((E, D, D_FF), D ** -0.5),
        'ev_ffn_w_up': nrm((E, D, D_FF), D ** -0.5),
        'ev_ffn_w_down': nrm((E, D_FF, D), D_FF ** -0.5 * res),
        'od_norm_mix': gain((O, D)),
        'od_w_in': nrm((O, D, ODD_IN), D ** -0.5),
        'od_rel_bias': nrm((O, CA_HEADS, 2 * REL_CLIP + 1), 0.5),
        'od_sgu_norm_g': gain((O, SGU_GROUPS, SGU_CH)),
        'od_sgu_norm_b': nrm((O, SGU_GROUPS, SGU_CH), 0.02),
        'od_sgu_w': nrm((O, SGU_GROUPS, SGU_CHUNK, SGU_CHUNK), SGU_CHUNK ** -0.5),
        'od_sgu_b': gain((O, SGU_GROUPS, SGU_CHUNK)),
        'od_w_out': nrm((O, ODD_MIX, D), ODD_MIX ** -0.5 * res),
        'od_norm_ffn': gain((O, D)),
        'od_router': nrm((O, D, N_EXPERTS), D ** -0.5),
        'od_moe_w_gate': nrm((O, N_EXPERTS, D, EXPERT_FF), D ** -0.5),
        'od_moe_w_up': nrm((O, N_EXPERTS, D, EXPERT_FF), D ** -0.5),
        'od_moe_w_down': nrm((O, N_EXPERTS, EXPERT_FF, D), EXPERT_FF ** -0.5 * res),
        'final_norm': gain((D,)),
    }

def reference(x, ev_norm_mix, ev_w_in, ev_pool_w, ev_pool_scale, ev_q_norm, ev_w_q_up, ev_kv_norm,
              ev_w_kv_up, ev_w_out, ev_norm_ffn, ev_ffn_w_gate, ev_ffn_w_up, ev_ffn_w_down,
              od_norm_mix, od_w_in, od_rel_bias, od_sgu_norm_g, od_sgu_norm_b, od_sgu_w, od_sgu_b,
              od_w_out, od_norm_ffn, od_router, od_moe_w_gate, od_moe_w_up, od_moe_w_down, final_norm):
    cos, sin = rope_tables(x.shape[1])
    for layer in range(DEPTH):
        i = layer // 2
        if layer % 2 == 0:
            h = rms_norm(x, ev_norm_mix[i])
            x = x + even_mixer(h, ev_w_in[i], ev_pool_w[i], ev_pool_scale[i], ev_q_norm[i], ev_w_q_up[i],
                               ev_kv_norm[i], ev_w_kv_up[i], ev_w_out[i], cos, sin)
            h = rms_norm(x, ev_norm_ffn[i])
            x = x + swiglu(h, ev_ffn_w_gate[i], ev_ffn_w_up[i], ev_ffn_w_down[i])
        else:
            h = rms_norm(x, od_norm_mix[i])
            x = x + odd_mixer(h, od_w_in[i], od_rel_bias[i], od_sgu_norm_g[i], od_sgu_norm_b[i],
                              od_sgu_w[i], od_sgu_b[i], od_w_out[i])
            h = rms_norm(x, od_norm_ffn[i])
            x = x + moe_swiglu(h, od_router[i], od_moe_w_gate[i], od_moe_w_up[i], od_moe_w_down[i])
    return rms_norm(x, final_norm)


_drawn_inputs = setup_inputs


def setup_inputs(seed=0):
    import zlib

    import numpy as np

    out = dict(_drawn_inputs(seed))
    spreads = {}
    factors = {'ev_q_norm': 8.0,
     'ev_kv_norm': 5.69,
     'od_sgu_norm_g': 3.647,
     'od_sgu_norm_b': 33.599,
     'ev_pool_scale': 2.969,
     'od_rel_bias': 3.827,
     'od_sgu_b': 4.108}
    for name, (base, spread) in spreads.items():
        noise = np.random.default_rng([zlib.crc32(name.encode()), seed]).standard_normal(out[name].shape)
        drawn = base * np.exp(spread * noise) if base else spread * noise
        out[name] = __import__('jax').numpy.asarray(drawn.astype(out[name].dtype))
    for name, factor in factors.items():
        out[name] = (out[name] * factor).astype(out[name].dtype)
    return out
```

```python
from contextlib import ExitStack

import numpy as np
import concourse.bass as bass
from concourse import mybir

F32 = mybir.dt.float32
F32R = mybir.dt.float32r
I32 = mybir.dt.int32
ALU = mybir.AluOpType
ACT = mybir.ActivationFunctionType
AX = mybir.AxisListType.X

P = 128
D = 1024
KD = D // P
SEQ = 256
TC = SEQ // P
HEADS = 8
EPS = 1e-6
NEG = -1e30

POOL_G, POOL_W = 4, (2, 4, 8, 16)
PAD = 16
A_W = 512
QR, KVR, ROPE = 256, 128, 32
LAT = QR + KVR + ROPE
NOPE, VD, DQ = 64, 64, 96
HR = ROPE // 2
FF = 2816
HD = 64
REL = 128
NE = 8
EFF = 3584

UNIT = 2048
RAW = 6
SPLIT = 3
SPLIT_D = 2
FFS = FF // 256
U_EVEN = 2 + 2 + 4
U_FFN = 3 * FFS
U_ODD = 10 + 4
U_DENSE = U_EVEN + U_FFN + U_ODD
JB = EFF // 512
U_EXP = 6 * JB
MORE = 3
ROUNDS = NE + MORE
assert U_EXP % RAW == 0 and U_EXP % SPLIT == 0

CONSTS = {}
_at = 0
for _n, _w in (("ident", P), ("tri", P), ("ones", P), ("causal", P), ("slot", P), ("mask0", P), ("mask1", 2 * P),
               ("cos", TC * HR), ("sin", TC * HR), ("invcnt", POOL_G * PAD), ("low", NE * NE), ("eidx", NE)):
    CONSTS[_n] = (_at, _at + _w)
    _at += _w
N_CONST = _at
PARAMS = {}
_at = 0
for _n, _w in (("g_mix0", KD), ("g_ffn0", KD), ("g_mix1", KD), ("g_ffn1", KD), ("pool_scale", POOL_G), ("q_norm", 2),
               ("kv_norm", 1), ("router", KD * NE), ("pool_w", POOL_G * P), ("sgu_w", POOL_G * P)):
    PARAMS[_n] = (_at, _at + _w)
    _at += _w
N_PARAM = _at
ROWS = {}
_at = 0
for _n, _w in (("sgu_b", 512), ("sgu_g", 512), ("sgu_nb", 512)):
    ROWS[_n] = (_at, _at + _w)
    _at += _w
N_ROW = _at


U_ODD0 = U_EVEN + U_FFN
PT_TILES = [(0, h, 0) for h in range(HEADS)] + [(1, h, kc) for h in range(HEADS) for kc in range(2)]
PT_BANK = (6, 7, 0, 1, 2, 3)


def FFN_GATE(step):
    return U_EVEN + (0 if step == 0 else 3 * step - 1)


def UP_END(j):
    return 3 if j == 0 else 6 * j + 1


def HT_AT(j):
    return min(6 * j + 7, U_EXP - 1)


def constants():
    c = np.zeros((P, N_CONST), np.float32)

    def put(name, value):
        a, b = CONSTS[name]
        c[:, a:b] = np.asarray(value, np.float32).reshape(P, b - a) if np.ndim(value) else value

    p, r = np.arange(P)[:, None], np.arange(P)[None, :]
    put("ident", p == r)
    put("tri", p < r)
    put("ones", 1.0)
    put("causal", p <= r)
    put("slot", np.broadcast_to(r + 1, (P, P)))
    keys = np.arange(2 * P)[None, :]
    put("mask0", np.where(r // 64 <= p // 64, 0.0, NEG))
    put("mask1", np.where(keys // 64 <= (P + p) // 64, 0.0, NEG))
    inv = (np.float32(1.0) / np.power(np.float32(10000.0), np.arange(0, ROPE, 2, dtype=np.float32) / np.float32(ROPE))).astype(np.float32)
    ang = (np.arange(SEQ, dtype=np.float32)[:, None] * inv[None, :]).astype(np.float32).astype(np.float64)
    put("cos", np.cos(ang).reshape(TC, P, HR).transpose(1, 0, 2).reshape(P, -1))
    put("sin", np.sin(ang).reshape(TC, P, HR).transpose(1, 0, 2).reshape(P, -1))
    t = np.arange(PAD)
    put("invcnt", np.broadcast_to(np.stack([1.0 / np.minimum(t + 1, w) for w in POOL_W]).reshape(1, -1), (P, POOL_G * PAD)))
    e = np.arange(NE)
    put("low", np.broadcast_to((e[None, :] < e[:, None]).reshape(1, -1), (P, NE * NE)))
    put("eidx", np.broadcast_to(e[None, :], (P, NE)))
    return c


def build(nc, t):
    ctx = ExitStack()
    with ctx:
        def sb(stack, name, shape, dt=F32):
            return stack.enter_context(nc.sbuf_tensor(name, shape, dt))

        def sem(name):
            return ctx.enter_context(nc.semaphore(name))

        raw = sb(ctx, "raw", [P, RAW, UNIT])
        cst = sb(ctx, "cst", [P, N_CONST])
        prm = sb(ctx, "prm", [P, N_PARAM])
        g_row = sb(ctx, "g_row", [P, D])
        x = sb(ctx, "x", [P, TC, D])
        ms = sb(ctx, "ms", [P, 5, TC])
        mse = sb(ctx, "mse", [P, 5, TC])
        std = sb(ctx, "std", [P, 5, TC])
        rstd = sb(ctx, "rstd", [P, 5, TC])
        warm = sb(ctx, "warm", [P, 2])
        lms = sb(ctx, "lms", [P, 2, TC])
        lmse = sb(ctx, "lmse", [P, 2, TC])
        lstd = sb(ctx, "lstd", [P, 2, TC])
        lrstd = sb(ctx, "lrstd", [P, 2, TC])
        gmean = sb(ctx, "gmean", [P, TC * POOL_G])
        gvar = sb(ctx, "gvar", [P, TC * POOL_G])
        gstd = sb(ctx, "gstd", [P, TC * POOL_G])
        grs = sb(ctx, "grs", [P, TC * POOL_G])
        mx = sb(ctx, "mx", [P, TC, HEADS])
        nmx = sb(ctx, "nmx", [P, TC, HEADS])
        sums = sb(ctx, "sums", [P, TC, HEADS])
        rec = sb(ctx, "rec", [P, TC, HEADS])
        lg = sb(ctx, "lg", [P, TC, NE])
        gt = sb(ctx, "gt", [P, TC * NE, NE])
        eq = sb(ctx, "eq", [P, TC * NE, NE])
        rank = sb(ctx, "rank", [P, TC, NE])
        chosen = sb(ctx, "chosen", [P, TC, NE])
        first = sb(ctx, "first", [P, TC, NE])
        second = sb(ctx, "second", [P, TC, NE])
        v1 = sb(ctx, "v1", [P, TC])
        v2 = sb(ctx, "v2", [P, TC])
        dv = sb(ctx, "dv", [P, TC])
        ev = sb(ctx, "ev", [P, TC])
        w1 = sb(ctx, "w1", [P, TC])
        w2 = sb(ctx, "w2", [P, TC])
        tmp8 = sb(ctx, "tmp8", [P, TC, NE])
        cnt = sb(ctx, "cnt", [P, NE])
        over = sb(ctx, "over", [P, NE])
        kx = sb(ctx, "kx", [P, NE])
        mj = sb(ctx, "mj", [P, MORE, NE])
        fold = sb(ctx, "fold", [P, TC, NE])
        info_f = sb(ctx, "info_f", [P, 1 + MORE])
        info = sb(ctx, "info", [P, 1 + MORE], I32)
        slot_of = sb(ctx, "slot_of", [P, ROUNDS + 1, TC])
        gate_of = sb(ctx, "gate_of", [P, ROUNDS + 1, TC])
        A_RING, A_QK, A_S, A_MIX, A_H, A_X = 0, 8192, 12288, 15360, 19456, 23552
        A_E = 25600
        A_END = A_E + 7680
        arena_base = nc.sbuf_base
        arena = sb(ctx, "arena", [P, A_END])
        assert arena_base % 32 == 0 and arena.name

        def at(name, shape, start, dt=F32):
            size = int(np.prod(shape[1:]))
            assert start % 8 == 0 and start + size <= A_END, name
            return nc.alloc_sbuf_tensor_at(name, shape, dt, offset=arena_base + 4 * start)

        dw_hi = at("dw_hi", [P, SPLIT_D, UNIT], A_RING, F32R)
        dw_lo = at("dw_lo", [P, SPLIT_D, UNIT], A_RING + SPLIT_D * UNIT, F32R)
        qT = at("qT", [P, HEADS, SEQ], A_QK)
        kT = at("kT", [P, HEADS, SEQ], A_QK + 2048)
        S0 = at("S0", [P, HEADS, P], A_S)
        S1 = at("S1", [P, HEADS, SEQ], A_S + 1024)
        mix_hi = at("mix_hi", [P, KD, SEQ], A_MIX, F32R)
        mix_lo = at("mix_lo", [P, KD, SEQ], A_MIX + 2048, F32R)
        hT_hi = at("hT_hi", [P, KD, SEQ], A_H, F32R)
        hT_lo = at("hT_lo", [P, KD, SEQ], A_H + 2048, F32R)
        PT = at("PT", [P, 3 * HEADS, P], A_H)
        hT = at("hT", [P, KD, SEQ], A_H)
        xn = at("xn", [P, TC, D], A_X)
        vv = at("vv", [P, TC, HEADS * VD], A_X)
        att = at("att", [P, TC, HEADS * VD], A_X + 1024)
        lat = at("lat", [P, TC, LAT], A_S)
        latn = at("latn", [P, TC, QR + KVR], A_S + 832)
        kr96 = at("kr96", [P, TC, DQ], A_S + 1600)
        ropek = at("ropek", [P, 4, TC, HR], A_S + 1792)
        latT = at("latT", [P, 3, SEQ], A_S + 1920)
        qq = at("qq", [P, TC, HEADS, DQ], A_S + 2688)
        ropeq = at("ropeq", [P, 4, TC * HEADS, HR], A_S + 4224)
        apad = at("apad", [P, POOL_G, PAD + SEQ], A_E)
        win1 = at("win1", [P, POOL_G, PAD + SEQ], A_E + 1088)
        win2 = at("win2", [P, POOL_G, PAD + SEQ], A_E + 2176)
        pooled = at("pooled", [P, POOL_G, SEQ], A_E + 3264)
        early = at("early", [P, POOL_G, PAD], A_E + 4288)
        wq_up = at("wq_up", [P, 2, HEADS * DQ], A_E + 4352)
        wkv_up = at("wkv_up", [P, HEADS * (NOPE + VD)], A_E + 5888)
        silu0 = at("silu0", [P, 2, 2 * SEQ], A_QK)
        hid0 = at("hid0", [P, 2, 2 * SEQ], A_QK + 1024)
        hid_hi = at("hid_hi", [P, 2, 2 * SEQ], A_QK + 2048, F32R)
        hid_lo = at("hid_lo", [P, 2, 2 * SEQ], A_QK + 3072, F32R)
        bias0 = at("bias0", [P, HEADS, P], A_E)
        bias1 = at("bias1", [P, HEADS, SEQ], A_E + 1024)
        rows = at("rows", [P, N_ROW], A_E + 3072)
        gv = at("gv", [P, TC * POOL_G, P], A_E + 4608)
        gsq = at("gsq", [P, TC * POOL_G, P], A_E + 5632)
        mixed = at("mixed", [P, POOL_G, SEQ], A_E + 5632)
        uT = at("uT", [P, POOL_G, SEQ], A_E + 6656)
        whi = at("whi", [P, SPLIT, UNIT], A_RING, F32R)
        wlo = at("wlo", [P, SPLIT, UNIT], A_RING + SPLIT * UNIT, F32R)
        y_hi = at("y_hi", [P, D], A_S, F32R)
        y_lo = at("y_lo", [P, D], A_S + 1024, F32R)
        pick = at("pick", [P, TC, P], A_S + 2048)
        pickr = at("pickr", [P, TC, P], A_S + 2304, F32R)
        place = at("place", [P, TC, P], A_S + 2560, F32R)
        h_hi = at("h_hi", [P, TC, D], A_MIX, F32R)
        h_lo = at("h_lo", [P, TC, D], A_MIX + 2048, F32R)
        xe_hi = at("xe_hi", [P, KD, P], A_E, F32R)
        xe_lo = at("xe_lo", [P, KD, P], A_E + 1024, F32R)
        sg = at("sg", [P, 2, 512], A_E + 2048)
        hid = at("hid", [P, 2, 512], A_E + 3072)
        ht_hi = at("ht_hi", [P, 2, 4, P], A_E + 4096, F32R)
        ht_lo = at("ht_lo", [P, 2, 4, P], A_E + 5120, F32R)
        g_final = at("g_final", [P, D], A_E + 6144)
        B = [ctx.enter_context(nc.psum_tensor(f"bank{i}", [P, 512], F32)) for i in range(8)]

        def x_bank(layer, k):
            return B[k // 2 + (0 if layer == 0 else 4)]

        def C(name):
            a, b = CONSTS[name]
            return cst[:, a:b]

        def PR(name):
            a, b = PARAMS[name]
            return prm[:, a:b]

        def RW(name):
            a, b = ROWS[name]
            return rows[:, a:b]

        consts_in, params_in, rows_in = sem("consts_in"), sem("params_in"), sem("rows_in")
        x_in = [sem(f"x_in{c}") for c in range(TC)]
        bias_in = sem("bias_in")
        raw_in = [sem(f"raw_in{s}") for s in range(RAW)]
        multiplied = sem("multiplied")
        x_ready = sem("x_ready")
        sq_done, mse_ready, std_ready, warm_ready = sem("sq_done"), sem("mse_ready"), sem("std_ready"), sem("warm_ready")
        xn_ready, xT_done = sem("xn_ready"), sem("xT_done")
        hT_act, hT_dve = sem("hT_act"), sem("hT_dve")
        c0_done = sem("c0_done")
        dchain, achain, pchain = sem("dchain"), sem("achain"), sem("pchain")
        lat_done, lat_copied, lsq_done, lmse_ready, lstd_ready = (sem("lat_done"), sem("lat_copied"), sem("lsq_done"), sem("lmse_ready"), sem("lstd_ready"))
        latn_ready, latT_done, latT_ready, kr_ready = sem("latn_ready"), sem("latT_done"), sem("latT_ready"), sem("kr_ready")
        a_done, a_padded, pads_zeroed, win_ready = sem("a_done"), sem("a_padded"), sem("pads_zeroed"), sem("win_ready")
        pooled_ready, pool_done, pool_mixed = sem("pooled_ready"), sem("pool_done"), sem("pool_mixed")
        q_done, q_copied, q_ready, qT_done, qT_ready = sem("q_done"), sem("q_copied"), sem("q_ready"), sem("qT_done"), sem("qT_ready")
        v_done, v_ready, k_done, k_ready = sem("v_done"), sem("v_ready"), sem("k_done"), sem("k_ready")
        kr96_zeroed, up_in, pool_hi = sem("kr96_zeroed"), sem("up_in"), sem("pool_hi")
        s_done, mx_ready, exp_done, pt_done, pt_act, pt_dve = (sem("s_done"), sem("mx_ready"), sem("exp_done"), sem("pt_done"), sem("pt_act"), sem("pt_dve"))
        pv_done, att_ready, attT_done, attT_hi, attT_ready = sem("pv_done"), sem("att_ready"), sem("attT_done"), sem("attT_hi"), sem("attT_ready")
        silu_ready, hid_made, hid_hi_ready, hid_ready = sem("silu_ready"), sem("hid_made"), sem("hid_hi_ready"), sem("hid_ready")
        bias_ready, qz_zeroed, oq_done, oq_ready, ok_done, ok_ready = (sem("bias_ready"), sem("qz_zeroed"), sem("oq_done"), sem("oq_ready"), sem("ok_done"), sem("ok_ready"))
        ov_done, ov_ready, ogv_done, gelu_gv, ou_done, gelu_u = (sem("ov_done"), sem("ov_ready"), sem("ogv_done"), sem("gelu_gv"), sem("ou_done"), sem("gelu_u"))
        gvar_ready, gstd_ready, vn_ready, wsT_ready, mixed_done, sg_made, sg_hi_ready, sg_ready = (sem("gvar_ready"), sem("gstd_ready"), sem("vn_ready"), sem("wsT_ready"), sem("mixed_done"), sem("sg_made"), sem("sg_hi_ready"), sem("sg_ready"))
        logits_done, dv_ready, ev_ready, chosen_ready, pos_done = sem("logits_done"), sem("dv_ready"), sem("ev_ready"), sem("chosen_ready"), sem("pos_done")
        route_ready, later_ready, tables_ready, rchain = sem("route_ready"), sem("later_ready"), sem("tables_ready"), sem("rchain")
        g_row_in, g_final_in = sem("g_row_in"), sem("g_final_in")
        hi_ready, lo_ready, hg_ready = sem("hi_ready"), sem("lo_ready"), sem("hg_ready")
        pick_ready, gathered, xe_hi_ready, xe_ready = sem("pick_ready"), sem("gathered"), sem("xe_hi_ready"), sem("xe_ready")
        placeT_done, place_ready = sem("placeT_done"), sem("place_ready")
        g_done, u_done, sg_ready_m, hid_ready_m = sem("g_done"), sem("u_done"), sem("moe_silu_ready"), sem("moe_hid_ready")
        hT_done_m, ht_hi_ready, ht_ready = sem("moe_hidT_done"), sem("ht_hi_ready"), sem("ht_ready")
        y_done, y_hi_ready, y_ready, y_zeroed = sem("y_done"), sem("y_hi_ready"), sem("y_ready"), sem("y_zeroed")
        h_hi_ready, h_lo_ready = sem("h_hi_ready"), sem("h_lo_ready")
        scattered, added = sem("scattered"), sem("added")
        final_ready, out_done = sem("final_ready"), sem("out_done")

        def unit_width(n):
            return dense_units[n].shape[1] * dense_units[n].shape[2]

        def rows_of(w, r0, nk, c0, c1):
            return w[r0:r0 + nk * P, c0:c1].rearrange("(k p) n -> p k n", p=P)

        dense_units = []
        w_in0, w_in1 = t["ev_w_in"], t["od_w_in"]
        for half in range(2):
            dense_units.append(rows_of(w_in0, half * 512, 4, A_W, A_W + LAT))
        for c in range(2):
            dense_units.append(rows_of(w_in0, 0, KD, c * 256, c * 256 + 256))
        for c in range(4):
            dense_units.append(rows_of(t["ev_w_out"], c * 256, 2, 0, D))
        for step in range(FFS + 1):
            if step < FFS:
                dense_units.append(rows_of(t["ev_ffn_w_gate"], 0, KD, step * 256, step * 256 + 256))
                dense_units.append(rows_of(t["ev_ffn_w_up"], 0, KD, step * 256, step * 256 + 256))
            if step:
                dense_units.append(rows_of(t["ev_ffn_w_down"], (step - 1) * 256, 2, 0, D))
        for c in range(4):
            dense_units.append(rows_of(w_in1, 0, KD, c * 256, c * 256 + 256))
        for part in (4, 2):
            for half in range(2):
                dense_units.append(rows_of(w_in1, half * 512, 4, part * 512, part * 512 + 512))
        for c in range(2):
            dense_units.append(rows_of(w_in1, 0, KD, 1536 + c * 256, 1536 + c * 256 + 256))
        for c in range(4):
            dense_units.append(rows_of(t["od_w_out"], c * 256, 2, 0, D))
        assert len(dense_units) == U_DENSE

        def expert_unit(kind, e, j, half):
            w = t["od_moe_w_" + kind]
            if kind == "down":
                r0 = j * 512 + half * 256
                return w[bass.ds(e, 1), r0:r0 + 256, :].rearrange("e (k p) n -> p (e k) n", p=P)
            return w[bass.ds(e, 1), half * 512:half * 512 + 512, j * 512:j * 512 + 512].rearrange("e (k p) n -> p (e k) n", p=P)

        order = []
        for j in range(JB):
            order += [("gate", j, 0), ("gate", j, 1), ("up", j, 0), ("up", j, 1)]
            if j:
                order += [("down", j - 1, 0), ("down", j - 1, 1)]
        order += [("down", JB - 1, 0), ("down", JB - 1, 1)]
        assert len(order) == U_EXP

        def landed(unit, rnd=0):
            n = unit // RAW + 1
            return raw_in[unit % RAW], 16 * (U_EXP // RAW) * rnd + 16 * n

        block = ctx.enter_context(nc.Block())

        @block.sync
        def _(sp):
            x_dram = t["x"].rearrange("b (c p) d -> p (b c) d", p=P)
            sp.dma_start(x[:, 0, :], x_dram[:, 0, :]).then_inc(x_in[0], 16)
            sp.dma_start(x[:, 1, :], x_dram[:, 1, :]).then_inc(x_in[1], 16)
            sp.dma_start(cst[:, :], t["consts"]).then_inc(consts_in, 16)
            for n, src in enumerate(dense_units):
                if n >= RAW:
                    sp.wait_ge(lo_ready, n - RAW + 1)
                k, w = src.shape[1], src.shape[2]
                dst = raw[:, n % RAW, 0:k * w].rearrange("p (k n) -> p k n", k=k)
                sp.dma_start(dst, src).then_inc(raw_in[n % RAW], 16)
                if n == 0:
                    sp.dma_start(prm[:, :], t["params"]).then_inc(params_in, 16)
                if n == 3:
                    sp.dma_start(wq_up[:, :, :], t["ev_w_q_up"].rearrange("(k p) n -> p k n", p=P)).then_inc(up_in, 16)
                    sp.dma_start(wkv_up[:, :], t["ev_w_kv_up"]).then_inc(up_in, 16)
                    sp.dma_start(g_row[:, :], t["g_ffn1"].partition_broadcast(P)).then_inc(g_row_in, 16)
                if n == U_EVEN + 12:
                    sp.dma_start(bias0[:, :, :], t["bias0"]).then_inc(bias_in, 16)
                    sp.dma_start(bias1[:, :, :], t["bias1"]).then_inc(bias_in, 16)
                    sp.dma_start(rows[:, :], t["rows"].partition_broadcast(P)).then_inc(rows_in, 16)

            def expert(e, rnd):
                for n, (kind, j, half) in enumerate(order):
                    u = U_DENSE + n
                    sp.wait_ge(lo_ready, rnd * U_EXP + (u - RAW + 1))
                    src = expert_unit(kind, e, j, half)
                    dst = raw[:, u % RAW, :].rearrange("p (k n) -> p k n", k=src.shape[1])
                    sp.dma_start(dst, src).then_inc(raw_in[u % RAW], 16)

            with sp.Fori(0, NE) as e:
                expert(e, e)
            sp.dma_start(g_final[:, :], t["g_final"].partition_broadcast(P)).then_inc(g_final_in, 16)
            sp.wait_ge(later_ready, 1)
            rounds = sp.value_load(info[0:1, 0:1], min_val=NE, max_val=ROUNDS)
            with sp.If(rounds > NE):
                with sp.Fori(NE, rounds) as rnd:
                    e = sp.value_load(info[0:1, bass.ds(rnd - (NE - 1), 1)], min_val=0, max_val=NE - 1)
                    expert(e, rnd)
            with sp.Else():
                sp.nop()
            for c in range(TC):
                sp.wait_ge(final_ready, c + 1)
                sp.dma_start(t["out"].rearrange("b (c p) d -> p (b c) d", p=P)[:, c, :], xn[:, c, :]).then_inc(out_done, 16)
            sp.wait_ge(out_done, 16 * TC)

        @block.gpsimd
        def _(pool):
            pool.memset(warm[:, :], 1.0).then_inc(warm_ready, 1)
            pool.memset(kr96[:, :, 0:NOPE], 0.0).then_inc(kr96_zeroed, 1)
            pool.memset(apad[:, :, 0:PAD], 0.0).then_inc(pads_zeroed, 1)
            pool.wait_ge(a_padded, 2)
            pool.wait_ge(pads_zeroed, 1)
            src, n = apad, PAD + SEQ
            for step in range(POOL_G):
                sh = 1 << step
                lo = 2 * sh - 1
                dst = (win1, win2)[step % 2]
                if step:
                    pool.wait_ge(win_ready, step)
                pool.tensor_tensor(dst[:, step:, lo:n], src[:, step:, lo:n], src[:, step:, lo - sh:n - sh], ALU.add).then_inc(win_ready, 1)
                src = dst
            pool.wait_ge(params_in, 16)
            pool.wait_ge(consts_in, 16)
            wsT = PR("sgu_w").rearrange("p (g t) -> p g t", g=POOL_G)
            pool.tensor_tensor(wsT, wsT, C("causal").unsqueeze(1).broadcast_to([P, POOL_G, P]), ALU.mult).then_inc(wsT_ready, 1)
            pool.wait_ge(bias_in, 32)
            pool.tensor_tensor(bias0[:, :, :], bias0[:, :, :], C("mask0").unsqueeze(1).broadcast_to([P, HEADS, P]), ALU.add).then_inc(bias_ready, 1)
            pool.tensor_tensor(bias1[:, :, :], bias1[:, :, :], C("mask1").unsqueeze(1).broadcast_to([P, HEADS, SEQ]), ALU.add).then_inc(bias_ready, 1)
            pool.wait_ge(multiplied, U_ODD0)
            pool.memset(qT[:, :, :], 0.0).then_inc(qz_zeroed, 1)
            pool.wait_ge(g_row_in, 16)
            for c in range(TC):
                pool.wait_ge(xT_done, 3 * TC + c + 1)
                pool.tensor_tensor(xn[:, c, :], xn[:, c, :], g_row[:, :], ALU.mult).then_inc(hg_ready, 1)
            steps = [0]

            def chain(ins):
                steps[0] += 1
                ins.then_inc(rchain, 1)
                pool.wait_ge(rchain, steps[0])

            def fold_into(out, buf):
                chain(pool.tensor_tensor(buf[:, :, 0:4], buf[:, :, 0:4], buf[:, :, 4:8], ALU.add))
                chain(pool.tensor_tensor(buf[:, :, 0:2], buf[:, :, 0:2], buf[:, :, 2:4], ALU.add))
                chain(pool.tensor_tensor(out, buf[:, :, 0], buf[:, :, 1], ALU.add))

            pool.wait_ge(tables_ready, 1)
            for j in range(MORE):
                mask = mj[:, j, :].unsqueeze(1).broadcast_to([P, TC, NE])
                chain(pool.tensor_tensor(fold[:, :, :], mask, slot_of[:, 0:NE, :].rearrange("p r c -> p c r"), ALU.mult))
                fold_into(slot_of[:, NE + j, :], fold)
                chain(pool.tensor_tensor(fold[:, :, :], mask, gate_of[:, 1:NE + 1, :].rearrange("p r c -> p c r"), ALU.mult))
                fold_into(gate_of[:, NE + 1 + j, :], fold)
                chain(pool.tensor_tensor(fold[:, 0:1, :], mj[:, j:j + 1, :], C("eidx").unsqueeze(1), ALU.mult))
                fold_into(info_f[:, 1 + j:2 + j], fold[:, 0:1, :])
            chain(pool.tensor_scalar(slot_of[:, NE:NE + MORE, :], slot_of[:, NE:NE + MORE, :], -float(P), None, ALU.add))
            pool.tensor_copy(info[:, 1:], info_f[:, 1:]).then_inc(later_ready, 1)

        @block.tensor
        def _(pe):
            mm, tr = nc.tensor.matmul, nc.tensor.transpose
            pe.wait_ge(consts_in, 16)
            ident = C("ident")
            unit_no = [0]

            def take(k, w):
                n = unit_no[0]
                unit_no[0] += 1
                pe.wait_ge(lo_ready, n + 1)
                return [v[:, n % SPLIT_D, 0:k * w].rearrange("p (k n) -> p k n", k=k) for v in (dw_hi, dw_lo)]

            def product(out, a, b, first, last):
                mm(out, a[0], b[0], start=first, stop=False)
                mm(out, a[0], b[1], start=False, stop=False)
                return mm(out, a[1], b[0], start=False, stop=last)

            def transpose_x(layer):
                for c in range(TC):
                    pe.wait_ge(xn_ready, TC * layer + c + 1)
                    for k in range(KD):
                        last = tr(x_bank(layer, k)[:, (k % 2) * SEQ + c * P:(k % 2) * SEQ + c * P + P], xn[:, c, k * P:(k + 1) * P], ident)
                    last.then_inc(xT_done, 1)

            def tokens_major(layer, banks, width):
                for half in range(2):
                    w = take(4, width)
                    for c in range(TC):
                        for k in range(4):
                            kk = half * 4 + k
                            pe.wait_ge(hT_dve, KD * layer + kk + 1)
                            last = product(banks[c][:, 0:width], [h[:, kk, c * P:(c + 1) * P] for h in (hT_hi, hT_lo)], [v[:, k, :] for v in w],
                                           kk == 0, kk == KD - 1)
                    last.then_inc(multiplied, 1)

            def features_major(layer, bank):
                w = take(KD, 256)
                for m in range(2):
                    for k in range(KD):
                        pe.wait_ge(hT_dve, KD * layer + k + 1)
                        last = product(bank[:, m * SEQ:(m + 1) * SEQ], [v[:, k, m * P:(m + 1) * P] for v in w], [h[:, k, :] for h in (hT_hi, hT_lo)],
                                       k == 0, k == KD - 1)
                last.then_inc(multiplied, 1)

            def back_to_width(n, units, chunk_of):
                w = take(2, D)
                for c in range(TC):
                    for k in range(2):
                        for half in range(2):
                            last = product(B[2 * c + half][:, :], chunk_of(k, c), [v[:, k, half * 512:(half + 1) * 512] for v in w],
                                           n == 0 and k == 0, n == units - 1 and k == 1)
                    if c == 0 and n == units - 1:
                        last.then_inc(c0_done, 1)
                last.then_inc(multiplied, 1)

            def project_out():
                for n in range(4):
                    back_to_width(n, 4, lambda k, c: [v[:, 2 * n + k, c * P:(c + 1) * P] for v in (mix_hi, mix_lo)])

            def scores(q_of, k_of):
                for h in range(HEADS):
                    last = mm(B[h // 4][:, (h % 4) * P:(h % 4 + 1) * P], q_of(h)[:, 0:P], k_of(h)[:, 0:P], start=True, stop=True)
                last.then_inc(s_done, 1)
                for h in range(HEADS):
                    last = mm(B[2 + h // 2][:, (h % 2) * SEQ:(h % 2 + 1) * SEQ], q_of(h)[:, P:SEQ], k_of(h)[:, 0:SEQ], start=True, stop=True)
                last.then_inc(s_done, 1)

            def values(layer):
                for b in range(6):
                    pe.wait_ge(exp_done, 16 * layer + (4 * (b + 1) if b < 2 else 8 + 2 * (b - 1)))
                    for n, (c, h, kc) in enumerate(PT_TILES[4 * b:4 * b + 4]):
                        src = S0[:, h, :] if c == 0 else S1[:, h, kc * P:(kc + 1) * P]
                        last = tr(B[PT_BANK[b]][:, n * P:(n + 1) * P], src, ident)
                    last.then_inc(pt_done, 1)
                for c in range(TC):
                    pe.wait_ge(pt_act, 3 * layer + (1 if c == 0 else 3))
                    pe.wait_ge(pt_dve, 3 * layer + (1 if c == 0 else 3))
                    for h in range(HEADS):
                        for kc in range(c + 1):
                            n = h if c == 0 else HEADS + 2 * h + kc
                            last = mm(B[6 + c][:, h * VD:(h + 1) * VD], PT[:, n, :], vv[:, kc, h * VD:(h + 1) * VD], start=(kc == 0), stop=(kc == c))
                    last.then_inc(pv_done, 1)
                for c in range(TC):
                    pe.wait_ge(att_ready, TC * layer + c + 1)
                    for m in range(4):
                        last = tr(B[m // 2][:, (m % 2) * SEQ + c * P:(m % 2) * SEQ + c * P + P], att[:, c, m * P:(m + 1) * P], ident)
                last.then_inc(attT_done, 1)
                pe.wait_ge(attT_ready, 2 * (layer + 1))

            pe.wait_ge(params_in, 16)
            transpose_x(0)
            tokens_major(0, (B[4], B[5]), LAT)
            features_major(0, B[6])
            features_major(0, B[7])
            pe.wait_ge(latn_ready, 3)
            pe.wait_ge(kr96_zeroed, 1)
            for c in range(TC):
                for m in range(2):
                    tr(B[0][:, m * SEQ + c * P:m * SEQ + c * P + P], latn[:, c, m * P:(m + 1) * P], ident)
                tr(B[1][:, c * P:(c + 1) * P], latn[:, c, QR:QR + KVR], ident)
                last = tr(B[1][0:DQ, SEQ + c * P:SEQ + (c + 1) * P], kr96[:, c, :], ident)
            last.then_inc(latT_done, 1)
            pe.wait_ge(latT_ready, 3)
            pe.wait_ge(up_in, 32)
            pe.wait_ge(lat_copied, 2)
            for c in range(TC):
                for half in range(2):
                    for k in range(2):
                        last = mm(B[2 + 2 * c + half][:, 0:4 * DQ], latT[:, k, c * P:(c + 1) * P], wq_up[:, k, half * 4 * DQ:(half + 1) * 4 * DQ],
                                  start=(k == 0), stop=(k == 1))
            last.then_inc(q_done, 1)
            wv = wkv_up[:, :].rearrange("p (h d) -> p h d", h=HEADS)
            pe.wait_ge(a_padded, 2)
            for c in range(TC):
                last = mm(B[6 + c][:, :].rearrange("p (h d) -> p h d", h=HEADS), latT[:, 2, c * P:(c + 1) * P], wv[:, :, NOPE:NOPE + VD], start=True, stop=True)
            last.then_inc(v_done, 1)
            pe.wait_ge(kr_ready, 1)
            for h in range(HEADS):
                if h == 4:
                    pe.wait_ge(q_copied, 4)
                last = mm(B[h // 2][0:NOPE, (h % 2) * SEQ:(h % 2 + 1) * SEQ], wv[:, h, 0:NOPE], latT[:, 2, :], start=True, stop=True)
                if h % 4 == 3:
                    last.then_inc(k_done, 1)
            pe.wait_ge(q_ready, 2)
            pe.wait_ge(k_ready, 4)
            for h in range(HEADS):
                for c in range(TC):
                    last = tr(B[h // 2][0:DQ, (h % 2) * SEQ + c * P:(h % 2) * SEQ + c * P + P], qq[:, c, h, :], ident)
                if h % 2:
                    last.then_inc(qT_done, 1)
            pe.wait_ge(qT_ready, 4)
            scores(lambda h: qT[0:DQ, h, :], lambda h: kT[0:DQ, h, :])
            pe.wait_ge(pooled_ready, 1)
            pe.wait_ge(v_ready, 2)
            pw = PR("pool_w").rearrange("p (g d) -> p g d", g=POOL_G)
            for g in range(POOL_G):
                last = mm(B[6 + g // 2][:, (g % 2) * SEQ:(g % 2 + 1) * SEQ], pw[:, g, :], pooled[:, g, :], start=True, stop=True)
            last.then_inc(pool_done, 1)
            pe.wait_ge(pool_mixed, 4)
            values(0)
            project_out()
            transpose_x(1)
            pe.wait_ge(hT_dve, KD + 2)
            for step in range(FFS + 1):
                if step < FFS:
                    if step >= 2:
                        pe.wait_ge(hid_made, step - 1)
                    features_major(1, B[4 + 2 * (step % 2)])
                    features_major(1, B[5 + 2 * (step % 2)])
                if step:
                    pe.wait_ge(hid_ready, step)
                    b = (step - 1) % 2
                    back_to_width(step - 1, FFS, lambda k, c: [v[:, b, k * SEQ + c * P:k * SEQ + (c + 1) * P] for v in (hid_hi, hid_lo)])
            transpose_x(2)
            for c in range(4):
                features_major(2, B[c])
            tokens_major(2, (B[4], B[5]), 512)
            tokens_major(2, (B[6], B[7]), 512)
            pe.wait_ge(oq_ready, 4)
            for c in range(2):
                features_major(2, B[c])
            pe.wait_ge(vn_ready, 1)
            pe.wait_ge(wsT_ready, 1)
            wsT = PR("sgu_w").rearrange("p (g t) -> p g t", g=POOL_G)
            for g in range(POOL_G):
                for c in range(TC):
                    last = mm(B[4 + g // 2][:, (g % 2) * SEQ + c * P:(g % 2) * SEQ + c * P + P], gv[:, c * POOL_G + g, :], wsT[:, g, :], start=True, stop=True)
            last.then_inc(mixed_done, 1)
            pe.wait_ge(gelu_u, 2)
            pe.wait_ge(ok_ready, 2)
            pe.wait_ge(ov_ready, 2)
            pe.wait_ge(sg_made, 1)
            scores(lambda h: qT[:, h, :], lambda h: kT[:, h // 2, :])
            values(1)
            pe.wait_ge(sg_ready, 1)
            project_out()
            transpose_x(3)
            pe.wait_ge(hT_act, 3 * KD + 4)
            pe.wait_ge(hT_dve, 3 * KD + 4)
            router = PR("router").rearrange("p (k e) -> p k e", k=KD)
            for c in range(TC):
                for k in range(KD):
                    last = mm(B[0][:, c * NE:(c + 1) * NE], hT[:, k, c * P:(c + 1) * P], router[:, k, :], start=(k == 0), stop=(k == KD - 1))
            last.then_inc(logits_done, 1)
            pe.wait_ge(chosen_ready, 1)
            tri, ones = C("tri"), C("ones")
            mm(B[1][:, 0:NE], tri, chosen[:, 0, :], start=True, stop=True)
            mm(B[1][:, NE:2 * NE], tri, chosen[:, 1, :], start=True, stop=False)
            mm(B[1][:, NE:2 * NE], ones, chosen[:, 0, :], start=False, stop=True)
            mm(B[1][:, 2 * NE:3 * NE], ones, chosen[:, 0, :], start=True, stop=False)
            mm(B[1][:, 2 * NE:3 * NE], ones, chosen[:, 1, :], start=False, stop=True).then_inc(pos_done, 1)
            pe.wait_ge(route_ready, 1)
            rounds = pe.value_load(info[0:1, 0:1], min_val=NE, max_val=ROUNDS)

            def gather(rnd):
                pe.wait_ge(pick_ready, rnd * 4 + 4)
                for k in range(KD):
                    n = 0
                    for part in (h_hi, h_lo):
                        for c in range(TC):
                            last = mm(B[4 + k // 4][:, (k % 4) * P:(k % 4 + 1) * P], part[:, c, k * P:(k + 1) * P], pickr[:, c, :],
                                      start=(n == 0), stop=(n == 3))
                            n += 1
                    if k % 4 == 3:
                        last.then_inc(gathered, 1)

            def scatter(rnd):
                pe.wait_ge(y_ready, rnd * 2 + 2)
                pe.wait_ge(place_ready, rnd + 1)
                for c in range(TC):
                    for half in range(2):
                        mm(B[4 + 2 * c + half][:, :], place[:, c, :], y_hi[:, half * 512:(half + 1) * 512], start=True, stop=False)
                        mm(B[4 + 2 * c + half][:, :], place[:, c, :], y_lo[:, half * 512:(half + 1) * 512], start=False, stop=True).then_inc(scattered, 1)

            pe.wait_ge(h_hi_ready, 2)
            pe.wait_ge(h_lo_ready, 2)
            gather(0)
            with pe.Fori(0, rounds) as rnd:
                def unit(n):
                    pe.wait_ge(lo_ready, rnd * U_EXP + (U_DENSE + n + 1))
                    u = n % SPLIT
                    return whi[:, u, :], wlo[:, u, :]

                def project(bank, n):
                    for half in range(2):
                        hi, lo = unit(n + half)
                        for k in range(4):
                            kk = 4 * half + k
                            last = product(bank[:, :], (xe_hi[:, kk, :], xe_lo[:, kk, :]), (hi[:, k * 512:(k + 1) * 512], lo[:, k * 512:(k + 1) * 512]),
                                           kk == 0, kk == KD - 1)
                        last.then_inc(multiplied, 1)

                def project_down(j, n):
                    pe.wait_ge(ht_ready, rnd * JB + (j + 1))
                    for part in range(2):
                        hi, lo = unit(n + part)
                        for m in range(2):
                            f = 2 * part + m
                            for half in range(2):
                                a = m * D + half * 512
                                last = product(B[half][:, :], (ht_hi[:, j % 2, f, :], ht_lo[:, j % 2, f, :]), (hi[:, a:a + 512], lo[:, a:a + 512]),
                                               j == 0 and f == 0, j == JB - 1 and f == 3)
                        last.then_inc(multiplied, 1)

                def transpose_hidden(j):
                    pe.wait_ge(hid_ready_m, rnd * JB + (j + 1))
                    for f in range(4):
                        last = tr(B[6][:, f * P:(f + 1) * P], hid[:, j % 2, f * P:(f + 1) * P], ident)
                    last.then_inc(hT_done_m, 1)

                n = 0
                pe.wait_ge(xe_ready, rnd * 2 + 2)
                for j in range(JB):
                    if j == 1:
                        pe.wait_ge(added, rnd * 4 + 2)
                    if j >= 2:
                        pe.wait_ge(hid_ready_m, rnd * JB + (j - 1))
                    project(B[2 + 2 * (j % 2)], n)
                    n += 2
                    if j:
                        transpose_hidden(j - 1)
                    project(B[3 + 2 * (j % 2)], n)
                    n += 2
                    if j == 0:
                        scatter(rnd)
                        pe.wait_ge(added, rnd * 4 + 4)
                        for c in range(TC):
                            last = tr(B[7][:, c * P:(c + 1) * P], pick[:, c, :], ident)
                        last.then_inc(placeT_done, 1)
                    else:
                        project_down(j - 1, n)
                        n += 2
                transpose_hidden(JB - 1)
                gather(rnd + 1)
                project_down(JB - 1, n)
            scatter(rounds)

        @block.scalar
        def _(act):
            A = nc.scalar.activation
            steps = [0]

            def chain(ins):
                steps[0] += 1
                ins.then_inc(achain, 1)
                act.wait_ge(achain, steps[0])

            split_no = [0]

            def split_to(n):
                while split_no[0] <= n:
                    u = split_no[0]
                    split_no[0] += 1
                    s, v = landed(u)
                    act.wait_ge(s, v)
                    if u >= SPLIT_D:
                        act.wait_ge(multiplied, u - SPLIT_D + 1)
                    w = unit_width(u)
                    A(dw_hi[:, u % SPLIT_D, 0:w], raw[:, u % RAW, 0:w], ACT.Copy).then_inc(hi_ready, 1)

            def load_table(func):
                act.wait_ge(warm_ready, 1)
                chain(A(warm[:, 1:2], warm[:, 0:1], func))

            def mean_square(layer):
                load_table(ACT.Sqrt)
                for c in range(TC):
                    if layer == 0:
                        act.wait_ge(x_in[c], 16)
                    elif layer < 4:
                        act.wait_ge(x_ready, 4 * layer - 2 + 2 * c)
                    A(xn[:, c, :], x[:, c, :], ACT.Square, scale=D ** -0.5, accum_out=ms[:, layer, c:c + 1]).then_inc(sq_done, 1)
                    act.wait_ge(mse_ready, TC * layer + c + 1)
                    A(std[:, layer, c:c + 1], mse[:, layer, c:c + 1], ACT.Sqrt).then_inc(std_ready, 1)

            def norm(layer, gain, ahead, func):
                mean_square(layer)
                split_to(ahead)
                act.wait_ge(xT_done, TC * (layer + 1))
                for k in range(KD):
                    A(hT_hi[:, k, :], x_bank(layer, k)[:, (k % 2) * SEQ:(k % 2 + 1) * SEQ], ACT.Copy, scale=PR(gain)[:, k:k + 1]).then_inc(hT_act, 1)
                load_table(func)

            def softmax(layer):
                for c in range(TC):
                    act.wait_ge(mx_ready, TC * layer + c + 1)
                    for h in range(HEADS):
                        s = S0[:, h, :] if c == 0 else S1[:, h, :]
                        A(s, s, ACT.Exp, bias=nmx[:, c, h:h + 1], accum_out=sums[:, c, h:h + 1]).then_inc(exp_done, 1)
                    if c == 0:
                        probs_out(layer, 1)
                probs_out(layer, 3)
                probs_out(layer, 5)

            def probs_out(layer, b):
                act.wait_ge(pt_done, 6 * layer + b + 1)
                A(PT[:, 4 * b:4 * b + 4, :], B[PT_BANK[b]][:, :].rearrange("p (n q) -> p n q", n=4), ACT.Copy).then_inc(pt_act, 1)

            def mix_out(layer, c0):
                act.wait_ge(attT_done, layer + 1)
                for b in range(2):
                    A(mix_hi[:, c0 + 2 * b:c0 + 2 * b + 2, :], B[b][:, :].rearrange("p (m t) -> p m t", m=2), ACT.Copy).then_inc(attT_hi, 1)

            act.wait_ge(params_in, 16)
            norm(0, "g_mix0", 0, ACT.Sqrt)
            split_to(2)
            act.wait_ge(multiplied, 2)
            for c in range(TC):
                A(lat[:, c, :], B[4 + c][:, 0:LAT], ACT.Copy).then_inc(lat_copied, 1)
            act.wait_ge(lat_copied, 2)
            for c in range(TC):
                A(latn[:, c, 0:QR], lat[:, c, 0:QR], ACT.Square, scale=QR ** -0.5, accum_out=lms[:, 0, c:c + 1]).then_inc(lsq_done, 1)
                A(latn[:, c, QR:QR + KVR], lat[:, c, QR:QR + KVR], ACT.Square, scale=KVR ** -0.5, accum_out=lms[:, 1, c:c + 1]).then_inc(lsq_done, 1)
            split_to(3)
            act.wait_ge(lmse_ready, 1)
            A(lstd[:, :, :], lmse[:, :, :], ACT.Sqrt).then_inc(lstd_ready, 1)
            load_table(ACT.Exp)
            for b in range(2):
                act.wait_ge(multiplied, 3 + b)
                A(apad[:, 2 * b:2 * b + 2, PAD:], B[6 + b][:, :].rearrange("p (g t) -> p g t", g=2), ACT.Copy).then_inc(a_padded, 1)
                split_to(4 + b)
            act.wait_ge(q_done, 1)
            for c in range(TC):
                for half in range(2):
                    A(qq[:, c, half * 4:(half + 1) * 4, :], B[2 + 2 * c + half][:, 0:4 * DQ].rearrange("p (h d) -> p h d", h=4), ACT.Copy).then_inc(q_copied, 1)
            for b in range(4):
                act.wait_ge(k_done, 1 + b // 2)
                A(kT[0:NOPE, 2 * b:2 * b + 2, :], B[b][0:NOPE, :].rearrange("p (h t) -> p h t", h=2), ACT.Copy).then_inc(k_ready, 1)
            act.wait_ge(pool_done, 1)
            for g in range(POOL_G):
                A(mix_hi[:, g, :], B[6 + g // 2][:, (g % 2) * SEQ:(g % 2 + 1) * SEQ], ACT.Copy, scale=PR("pool_scale")[:, g:g + 1]).then_inc(pool_hi, 1)
            softmax(0)
            mix_out(0, 4)
            split_to(U_EVEN)
            norm(1, "g_ffn0", U_EVEN + 1, ACT.Silu)
            for step in range(FFS):
                gate = FFN_GATE(step)
                split_to(gate + 1)
                act.wait_ge(multiplied, gate + 1)
                if step >= 2:
                    act.wait_ge(hid_made, step - 1)
                A(silu0[:, step % 2, :], B[4 + 2 * (step % 2)][:, :], ACT.Silu).then_inc(silu_ready, 1)
                split_to(gate + 3 if step else gate + 2)
                act.wait_ge(hid_made, step + 1)
                A(hid_hi[:, step % 2, :], hid0[:, step % 2, :], ACT.Copy).then_inc(hid_hi_ready, 1)
            split_to(U_ODD0)
            norm(2, "g_mix1", U_ODD0 + 1, ACT.Gelu_apprx_tanh)
            for b in range(2):
                split_to(U_ODD0 + 3 + b)
                act.wait_ge(multiplied, U_ODD0 + 3 + b)
                A(kT[:, 2 * b:2 * b + 2, :], B[2 + b][:, :].rearrange("p (m t) -> p m t", m=2), ACT.Copy).then_inc(ok_ready, 1)
            split_to(U_ODD0 + 6)
            act.wait_ge(multiplied, U_ODD0 + 6)
            for c in range(TC):
                A(gv[:, c * POOL_G:(c + 1) * POOL_G, :], B[4 + c][:, :].rearrange("p (g d) -> p g d", g=POOL_G), ACT.Gelu_apprx_tanh).then_inc(gelu_gv, 1)
            split_to(U_ODD0 + 8)
            act.wait_ge(gvar_ready, 1)
            A(gstd[:, :], gvar[:, :], ACT.Sqrt).then_inc(gstd_ready, 1)
            load_table(ACT.Gelu_apprx_tanh)
            act.wait_ge(multiplied, U_ODD0 + 8)
            for c in range(TC):
                A(vv[:, c, :], B[6 + c][:, :], ACT.Copy).then_inc(ov_ready, 1)
            for b in range(2):
                split_to(U_ODD0 + 9 + b)
                act.wait_ge(multiplied, U_ODD0 + 9 + b)
                A(uT[:, 2 * b:2 * b + 2, :], B[b][:, :].rearrange("p (g t) -> p g t", g=2), ACT.Gelu_apprx_tanh).then_inc(gelu_u, 1)
            split_to(U_ODD0 + 11)
            load_table(ACT.Exp)
            act.wait_ge(sg_made, 1)
            A(mix_hi[:, 4:8, :], mixed[:, :, :], ACT.Copy).then_inc(sg_hi_ready, 1)
            softmax(1)
            mix_out(1, 0)
            split_to(U_DENSE - 1)
            mean_square(3)
            act.wait_ge(xT_done, TC * 4)
            for k in range(4):
                A(hT[:, k, :], x_bank(3, k)[:, (k % 2) * SEQ:(k % 2 + 1) * SEQ], ACT.Copy, scale=PR("g_ffn1")[:, k:k + 1]).then_inc(hT_act, 1)
            for c in range(TC):
                act.wait_ge(hg_ready, c + 1)
                A(h_hi[:, c, :], xn[:, c, :], ACT.Copy).then_inc(h_hi_ready, 1)
            load_table(ACT.Exp)
            act.wait_ge(dv_ready, 1)
            A(ev[:, :], dv[:, :], ACT.Exp).then_inc(ev_ready, 1)
            load_table(ACT.Silu)
            act.wait_ge(route_ready, 1)
            rounds = act.value_load(info[0:1, 0:1], min_val=NE, max_val=ROUNDS)

            def packed_out(rnd):
                for b in range(2):
                    act.wait_ge(gathered, rnd * 2 + (b + 1))
                    A(xe_hi[:, 4 * b:4 * b + 4, :], B[4 + b][:, :].rearrange("p (k s) -> p k s", k=4), ACT.Copy).then_inc(xe_hi_ready, 1)

            def result_out():
                for half in range(2):
                    A(y_hi[:, half * 512:(half + 1) * 512], B[half][:, :], ACT.Copy).then_inc(y_hi_ready, 1)

            packed_out(0)
            with act.Fori(0, rounds) as rnd:
                for n in range(U_EXP):
                    s, v = landed(U_DENSE + n)
                    act.wait_ge(s, rnd * (16 * U_EXP // RAW) + v)
                    act.wait_ge(multiplied, rnd * U_EXP + (U_DENSE + n - SPLIT + 1))
                    A(whi[:, n % SPLIT, :], raw[:, (U_DENSE + n) % RAW, :], ACT.Copy).then_inc(hi_ready, 1)
                    if n == 1:
                        act.wait_ge(multiplied, rnd * U_EXP + U_DENSE)
                        act.wait_ge(y_zeroed, 2)
                        result_out()
                    for j in range(JB):
                        if n == UP_END(j) + 2:
                            act.wait_ge(multiplied, rnd * U_EXP + (U_DENSE + UP_END(j) - 1))
                            if j >= 2:
                                act.wait_ge(hid_ready_m, rnd * JB + (j - 1))
                            A(sg[:, j % 2, :], B[2 + 2 * (j % 2)][:, :], ACT.Silu).then_inc(sg_ready_m, 1)
                        if n == HT_AT(j):
                            act.wait_ge(hT_done_m, rnd * JB + (j + 1))
                            A(ht_hi[:, j % 2, :, :], B[6][:, :].rearrange("p (f s) -> p f s", f=4), ACT.Copy).then_inc(ht_hi_ready, 1)
                    if n == UP_END(0) + 2:
                        act.wait_ge(placeT_done, rnd + 1)
                        A(place[:, :, :], B[7][:, 0:TC * P].rearrange("p (c t) -> p c t", c=TC), ACT.Copy).then_inc(place_ready, 1)
                packed_out(rnd + 1)
            act.wait_ge(multiplied, rounds * U_EXP + U_DENSE)
            result_out()
            act.wait_ge(added, rounds * 4 + 4)
            mean_square(4)

        @block.vector
        def _(dve):
            V = nc.vector
            steps = [0]

            def chain(ins):
                steps[0] += 1
                ins.then_inc(dchain, 1)
                dve.wait_ge(dchain, steps[0])

            split_no = [0]

            def split_to(n):
                while split_no[0] <= n:
                    u = split_no[0]
                    split_no[0] += 1
                    dve.wait_ge(hi_ready, u + 1)
                    w = unit_width(u)
                    V.tensor_tensor(dw_lo[:, u % SPLIT_D, 0:w], raw[:, u % RAW, 0:w], dw_hi[:, u % SPLIT_D, 0:w].bitcast(F32),
                                    ALU.subtract).then_inc(lo_ready, 1)

            def rstd_of(layer, c):
                dve.wait_ge(sq_done, TC * layer + c + 1)
                V.tensor_scalar(mse[:, layer, c:c + 1], ms[:, layer, c:c + 1], EPS, None, ALU.add).then_inc(mse_ready, 1)
                dve.wait_ge(std_ready, TC * layer + c + 1)
                chain(V.reciprocal(rstd[:, layer, c:c + 1], std[:, layer, c:c + 1]))

            def normalise(layer, units=None):
                for c in range(TC):
                    if units is not None:
                        dve.wait_ge(*((c0_done, layer) if c == 0 else (multiplied, units)))
                        for half in range(2):
                            xs = x[:, c, half * 512:(half + 1) * 512]
                            V.tensor_tensor(xs, B[2 * c + half][:, :], xs, ALU.add).then_inc(x_ready, 1)
                        dve.wait_ge(x_ready, 4 * layer - 2 + 2 * c)
                    rstd_of(layer, c)
                    V.tensor_scalar(xn[:, c, :], x[:, c, :], rstd[:, layer, c:c + 1], None, ALU.mult).then_inc(xn_ready, 1)

            def low_halves(layer, gain):
                for k in range(KD):
                    dve.wait_ge(hT_act, KD * layer + 2 * (k // 2) + 2)
                    V.scalar_tensor_tensor(hT_lo[:, k, :], x_bank(layer, k)[:, (k % 2) * SEQ:(k % 2 + 1) * SEQ], PR(gain)[:, k:k + 1],
                                           hT_hi[:, k, :].bitcast(F32), ALU.mult, ALU.subtract).then_inc(hT_dve, 1)

            def masked_scores(layer, scale, mask_of):
                for c in range(TC):
                    dve.wait_ge(s_done, TC * layer + c + 1)
                    dst, nk = (S0, P) if c == 0 else (S1, SEQ)
                    per = 512 // nk
                    for b in range(HEADS // per):
                        last = V.scalar_tensor_tensor(dst[:, b * per:(b + 1) * per, :], B[2 * c + b][:, :].rearrange("p (h k) -> p h k", h=per),
                                                      scale, mask_of(c, b * per, (b + 1) * per), ALU.mult, ALU.add)
                    chain(last)
                    chain(V.tensor_reduce(mx[:, c, :], dst[:, :, :], AX, ALU.max))
                    V.tensor_scalar(nmx[:, c, :], mx[:, c, :], -1.0, None, ALU.mult).then_inc(mx_ready, 1)

            def probs_out(layer, b):
                dve.wait_ge(pt_done, 6 * layer + b + 1)
                V.tensor_copy(PT[:, 4 * b:4 * b + 4, :], B[PT_BANK[b]][:, :].rearrange("p (n q) -> p n q", n=4)).then_inc(pt_dve, 1)

            def attention_out(layer, c0):
                probs_out(layer, 0)
                probs_out(layer, 2)
                probs_out(layer, 4)
                for c in range(TC):
                    dve.wait_ge(exp_done, 16 * layer + 8 * (c + 1))
                    chain(V.reciprocal(rec[:, c, :], sums[:, c, :]))
                    dve.wait_ge(pv_done, TC * layer + c + 1)
                    V.tensor_tensor(att[:, c, :].rearrange("p (h d) -> p h d", h=HEADS), B[6 + c][:, :].rearrange("p (h d) -> p h d", h=HEADS),
                                    rec[:, c, :].unsqueeze(2).broadcast_to([P, HEADS, VD]), ALU.mult).then_inc(att_ready, 1)
                for b in range(2):
                    dve.wait_ge(attT_hi, 2 * layer + b + 1)
                    rng = slice(c0 + 2 * b, c0 + 2 * b + 2)
                    V.tensor_tensor(mix_lo[:, rng, :], B[b][:, :].rearrange("p (m t) -> p m t", m=2), mix_hi[:, rng, :].bitcast(F32),
                                    ALU.subtract).then_inc(attT_ready, 1)

            def rotate(buf, x1, x2, cos, sin):
                V.tensor_tensor(buf[0], x1, cos, ALU.mult)
                V.tensor_tensor(buf[1], x2, sin, ALU.mult)
                V.tensor_tensor(buf[2], x2, cos, ALU.mult)
                chain(V.tensor_tensor(buf[3], x1, sin, ALU.mult))
                return buf

            dve.wait_ge(x_in[0], 16)
            dve.wait_ge(x_in[1], 16)
            dve.wait_ge(consts_in, 16)
            normalise(0)
            split_to(0)
            dve.wait_ge(params_in, 16)
            low_halves(0, "g_mix0")
            split_to(2)
            dve.wait_ge(lsq_done, 4)
            V.tensor_scalar(lmse[:, :, :], lms[:, :, :], EPS, None, ALU.add).then_inc(lmse_ready, 1)
            split_to(3)
            cos = C("cos").rearrange("p (c r) -> p c r", c=TC)
            sin = C("sin").rearrange("p (c r) -> p c r", c=TC)
            dve.wait_ge(lat_copied, 2)
            k1, k2 = lat[:, :, QR + KVR:QR + KVR + HR], lat[:, :, QR + KVR + HR:LAT]
            b4 = rotate([ropek[:, n, :, :] for n in range(4)], k1, k2, cos, sin)
            V.tensor_tensor(kr96[:, :, NOPE:NOPE + HR], b4[0], b4[1], ALU.subtract).then_inc(latn_ready, 1)
            V.tensor_tensor(kr96[:, :, NOPE + HR:DQ], b4[2], b4[3], ALU.add).then_inc(latn_ready, 1)
            dve.wait_ge(lstd_ready, 1)
            chain(V.reciprocal(lrstd[:, :, :], lstd[:, :, :]))
            for c in range(TC):
                V.tensor_scalar(latn[:, c, 0:QR], lat[:, c, 0:QR], lrstd[:, 0, c:c + 1], None, ALU.mult)
                last = V.tensor_scalar(latn[:, c, QR:QR + KVR], lat[:, c, QR:QR + KVR], lrstd[:, 1, c:c + 1], None, ALU.mult)
            last.then_inc(latn_ready, 1)
            split_to(5)
            dve.wait_ge(latT_done, 1)
            for m in range(2):
                V.tensor_scalar(latT[:, m, :], B[0][:, m * SEQ:(m + 1) * SEQ], PR("q_norm")[:, m:m + 1], None, ALU.mult).then_inc(latT_ready, 1)
            V.tensor_scalar(latT[:, 2, :], B[1][:, 0:SEQ], PR("kv_norm"), None, ALU.mult).then_inc(latT_ready, 1)
            V.tensor_copy(kT[NOPE:DQ, :, :], B[1][NOPE:DQ, SEQ:2 * SEQ].unsqueeze(1).broadcast_to([ROPE, HEADS, SEQ])).then_inc(kr_ready, 1)
            dve.wait_ge(v_done, 1)
            for c in range(TC):
                V.tensor_copy(vv[:, c, :], B[6 + c][:, :]).then_inc(v_ready, 1)
            dve.wait_ge(q_copied, 4)
            cosh, sinh = (a.unsqueeze(2).broadcast_to([P, TC, HEADS, HR]) for a in (cos, sin))
            q1, q2 = qq[:, :, :, NOPE:NOPE + HR], qq[:, :, :, NOPE + HR:DQ]
            b4 = rotate([ropeq[:, n, :, :].rearrange("p (c h) r -> p c h r", c=TC) for n in range(4)], q1, q2, cosh, sinh)
            V.tensor_tensor(q1, b4[0], b4[1], ALU.subtract).then_inc(q_ready, 1)
            V.tensor_tensor(q2, b4[2], b4[3], ALU.add).then_inc(q_ready, 1)
            for b in range(4):
                dve.wait_ge(qT_done, b + 1)
                V.tensor_copy(qT[0:DQ, 2 * b:2 * b + 2, :], B[b][0:DQ, :].rearrange("p (h t) -> p h t", h=2)).then_inc(qT_ready, 1)
            dve.wait_ge(win_ready, POOL_G)
            inv = C("invcnt").rearrange("p (g t) -> p g t", g=POOL_G)
            for g in range(POOL_G):
                win = (win1, win2)[g % 2]
                V.scalar_tensor_tensor(pooled[:, g, :], win[:, g, PAD:], 1.0 / POOL_W[g], apad[:, g, PAD:], ALU.mult, ALU.subtract)
                last = V.tensor_tensor(early[:, g, :], win[:, g, PAD:2 * PAD], inv[:, g, :], ALU.mult)
            chain(last)
            V.tensor_tensor(pooled[:, :, 0:PAD], early[:, :, :], apad[:, :, PAD:2 * PAD], ALU.subtract).then_inc(pooled_ready, 1)
            for g in range(POOL_G):
                dve.wait_ge(pool_hi, 2 * (g // 2) + 2)
                V.scalar_tensor_tensor(mix_lo[:, g, :], B[6 + g // 2][:, (g % 2) * SEQ:(g % 2 + 1) * SEQ], PR("pool_scale")[:, g:g + 1],
                                       mix_hi[:, g, :].bitcast(F32), ALU.mult, ALU.subtract).then_inc(pool_mixed, 1)
            masked_scores(0, DQ ** -0.5, lambda c, h0, h1: C(f"mask{c}").unsqueeze(1).broadcast_to([P, h1 - h0, P * (c + 1)]))
            attention_out(0, 4)
            split_to(U_EVEN)
            normalise(1, U_EVEN)
            split_to(U_EVEN + 1)
            low_halves(1, "g_ffn0")
            for step in range(FFS):
                gate = FFN_GATE(step)
                split_to(gate + 2)
                dve.wait_ge(silu_ready, step + 1)
                dve.wait_ge(multiplied, gate + 2)
                if step >= 2:
                    dve.wait_ge(hid_hi_ready, step - 1)
                V.tensor_tensor(hid0[:, step % 2, :], silu0[:, step % 2, :], B[5 + 2 * (step % 2)][:, :], ALU.mult).then_inc(hid_made, 1)
                split_to(gate + 3 if step else gate + 2)
                dve.wait_ge(hid_hi_ready, step + 1)
                V.tensor_tensor(hid_lo[:, step % 2, :], hid0[:, step % 2, :], hid_hi[:, step % 2, :].bitcast(F32), ALU.subtract).then_inc(hid_ready, 1)
            split_to(U_ODD0)
            normalise(2, U_ODD0)
            split_to(U_ODD0 + 1)
            low_halves(2, "g_mix1")
            dve.wait_ge(qz_zeroed, 1)
            for b in range(2):
                split_to(U_ODD0 + 1 + b)
                dve.wait_ge(multiplied, U_ODD0 + 1 + b)
                src = B[b][:, :].rearrange("p (m t) -> p m t", m=2)
                V.tensor_copy(qT[0:HD, 4 * b:4 * b + 4:2, :], src[0:HD]).then_inc(oq_ready, 1)
                V.tensor_copy(qT[HD:P, 4 * b + 1:4 * b + 4:2, :], src[HD:P]).then_inc(oq_ready, 1)
            split_to(U_ODD0 + 6)
            dve.wait_ge(gelu_gv, 2)
            wide = [P, TC * POOL_G, P]
            chain(V.tensor_reduce(gmean[:, :], gv[:, :, :], AX, ALU.add))
            chain(V.tensor_scalar(gmean[:, :], gmean[:, :], -1.0 / P, None, ALU.mult))
            split_to(U_ODD0 + 7)
            chain(V.tensor_tensor(gv[:, :, :], gv[:, :, :], gmean[:, :].unsqueeze(2).broadcast_to(wide), ALU.add))
            chain(V.tensor_tensor(gsq[:, :, :], gv[:, :, :], gv[:, :, :], ALU.mult))
            chain(V.tensor_reduce(gvar[:, :], gsq[:, :, :], AX, ALU.add))
            V.tensor_scalar(gvar[:, :], gvar[:, :], 1.0 / P, EPS, ALU.mult, ALU.add).then_inc(gvar_ready, 1)
            split_to(U_ODD0 + 8)
            dve.wait_ge(gstd_ready, 1)
            chain(V.reciprocal(grs[:, :], gstd[:, :]))
            chain(V.tensor_tensor(gv[:, :, :], gv[:, :, :], grs[:, :].unsqueeze(2).broadcast_to(wide), ALU.mult))
            split_to(U_ODD0 + 9)
            dve.wait_ge(rows_in, 16)
            gv2 = gv[:, :, :].rearrange("p (c g) d -> p c (g d)", c=TC)
            chain(V.tensor_tensor(gv2, gv2, RW("sgu_g").unsqueeze(1).broadcast_to([P, TC, 512]), ALU.mult))
            V.tensor_tensor(gv2, gv2, RW("sgu_nb").unsqueeze(1).broadcast_to([P, TC, 512]), ALU.add).then_inc(vn_ready, 1)
            split_to(U_ODD0 + 11)
            dve.wait_ge(mixed_done, 1)
            sb_row = RW("sgu_b").rearrange("p (g t) -> p g t", g=POOL_G)
            for b in range(2):
                last = V.tensor_tensor(mixed[:, 2 * b:2 * b + 2, :].rearrange("p g (c t) -> p g c t", c=TC),
                                       B[4 + b][:, :].rearrange("p (g c t) -> p g c t", g=2, c=TC),
                                       sb_row[:, 2 * b:2 * b + 2, :].unsqueeze(2).broadcast_to([P, 2, TC, P]), ALU.add)
            chain(last)
            dve.wait_ge(gelu_u, 2)
            V.tensor_tensor(mixed[:, :, :], mixed[:, :, :], uT[:, :, :], ALU.mult).then_inc(sg_made, 1)
            dve.wait_ge(sg_hi_ready, 1)
            V.tensor_tensor(mix_lo[:, 4:8, :], mixed[:, :, :], mix_hi[:, 4:8, :].bitcast(F32), ALU.subtract).then_inc(sg_ready, 1)
            dve.wait_ge(bias_ready, 2)
            masked_scores(1, HD ** -0.5, lambda c, h0, h1: (bias0, bias1)[c][:, h0:h1, :])
            attention_out(1, 0)
            split_to(U_DENSE - 1)
            normalise(3, U_DENSE)
            dve.wait_ge(xT_done, TC * 4)
            for k in range(4, KD):
                V.tensor_scalar(hT[:, k, :], x_bank(3, k)[:, (k % 2) * SEQ:(k % 2 + 1) * SEQ], PR("g_ffn1")[:, k:k + 1], None, ALU.mult).then_inc(hT_dve, 1)
            dve.wait_ge(logits_done, 1)
            chain(V.tensor_copy(lg[:, :, :], B[0][:, 0:TC * NE].rearrange("p (c e) -> p c e", c=TC)))
            mine = lg[:, :, :].unsqueeze(3).broadcast_to([P, TC, NE, NE])
            other = lg[:, :, :].unsqueeze(2).broadcast_to([P, TC, NE, NE])
            gt4 = gt[:, :, :].rearrange("p (c e) f -> p c e f", c=TC)
            eq4 = eq[:, :, :].rearrange("p (c e) f -> p c e f", c=TC)
            low = C("low").rearrange("p (e f) -> p e f", e=NE)
            V.tensor_tensor(gt4, other, mine, ALU.is_gt)
            chain(V.tensor_tensor(eq4, other, mine, ALU.is_equal))
            chain(V.tensor_tensor(eq4, eq4, low.unsqueeze(1).broadcast_to([P, TC, NE, NE]), ALU.mult))
            chain(V.tensor_tensor(gt[:, :, :], gt[:, :, :], eq[:, :, :], ALU.add))
            chain(V.tensor_reduce(rank[:, :, :], gt4, AX, ALU.add))
            V.tensor_scalar(chosen[:, :, :], rank[:, :, :], 1.5, None, ALU.is_lt).then_inc(chosen_ready, 1)
            chain(V.tensor_scalar(first[:, :, :], rank[:, :, :], 0.5, None, ALU.is_lt))
            V.tensor_tensor(second[:, :, :], chosen[:, :, :], first[:, :, :], ALU.subtract)
            chain(V.tensor_tensor(tmp8[:, :, :], first[:, :, :], lg[:, :, :], ALU.mult))
            chain(V.tensor_reduce(v1[:, :], tmp8[:, :, :], AX, ALU.add))
            chain(V.tensor_tensor(tmp8[:, :, :], second[:, :, :], lg[:, :, :], ALU.mult))
            chain(V.tensor_reduce(v2[:, :], tmp8[:, :, :], AX, ALU.add))
            V.tensor_tensor(dv[:, :], v2[:, :], v1[:, :], ALU.subtract).then_inc(dv_ready, 1)
            V.memset(slot_of[:, NE + MORE:, :], 0.0)
            V.memset(gate_of[:, 0:1, :], 0.0)
            V.memset(place[:, :, :].bitcast(F32), 0.0).then_inc(place_ready, 1)
            dve.wait_ge(pos_done, 1)
            V.scalar_tensor_tensor(slot_of[:, 0:NE, :].rearrange("p r c -> p c r"), B[1][:, 0:TC * NE].rearrange("p (c e) -> p c e", c=TC),
                                   1.0, chosen[:, :, :], ALU.add, ALU.mult)
            chain(V.tensor_scalar(over[:, :], B[1][:, 2 * NE:3 * NE], P + 0.5, None, ALU.is_gt))
            chain(V.tensor_reduce(info_f[:, 0:1], over[:, :], AX, ALU.add))
            V.tensor_scalar(info[:, 0:1], info_f[:, 0:1], float(NE), None, ALU.add).then_inc(route_ready, 1)
            def picks(rnd):
                for c in range(TC):
                    col = slot_of[:, bass.ds(rnd, 1), c]
                    V.tensor_scalar(pick[:, c, :], C("slot"), col, None, ALU.is_equal).then_inc(pick_ready, 1)
                    V.tensor_scalar(pickr[:, c, :], C("slot"), col, None, ALU.is_equal).then_inc(pick_ready, 1)

            def packed_out(rnd):
                for b in range(2):
                    dve.wait_ge(xe_hi_ready, rnd * 2 + (b + 1))
                    V.tensor_tensor(xe_lo[:, 4 * b:4 * b + 4, :], B[4 + b][:, :].rearrange("p (k s) -> p k s", k=4),
                                    xe_hi[:, 4 * b:4 * b + 4, :].bitcast(F32), ALU.subtract).then_inc(xe_ready, 1)

            def result_out(rnd):
                for half in range(2):
                    dve.wait_ge(y_hi_ready, rnd * 2 + (half + 1))
                    cols = slice(half * 512, (half + 1) * 512)
                    V.tensor_tensor(y_lo[:, cols], B[half][:, :], y_hi[:, cols].bitcast(F32), ALU.subtract).then_inc(y_ready, 1)

            def add_back(rnd):
                for c in range(TC):
                    for half in range(2):
                        dve.wait_ge(scattered, rnd * 4 + (2 * c + half + 1))
                        xs = x[:, c, half * 512:(half + 1) * 512]
                        V.scalar_tensor_tensor(xs, B[4 + 2 * c + half][:, :], gate_of[:, bass.ds(rnd, 1), c], xs, ALU.mult, ALU.add).then_inc(added, 1)

            picks(0)
            V.memset(B[0][:, :], 0.0).then_inc(y_zeroed, 1)
            V.memset(B[1][:, :], 0.0).then_inc(y_zeroed, 1)
            for c in range(TC):
                dve.wait_ge(h_hi_ready, c + 1)
                V.tensor_tensor(h_lo[:, c, :], xn[:, c, :], h_hi[:, c, :].bitcast(F32), ALU.subtract).then_inc(h_lo_ready, 1)
            dve.wait_ge(ev_ready, 1)
            chain(V.tensor_scalar(w1[:, :], ev[:, :], 1.0, None, ALU.add))
            chain(V.reciprocal(w1[:, :], w1[:, :]))
            chain(V.tensor_tensor(w2[:, :], ev[:, :], w1[:, :], ALU.mult))
            packed_out(0)
            V.tensor_tensor(first[:, :, :], first[:, :, :], w1[:, :].unsqueeze(2).broadcast_to([P, TC, NE]), ALU.mult)
            chain(V.tensor_tensor(second[:, :, :], second[:, :, :], w2[:, :].unsqueeze(2).broadcast_to([P, TC, NE]), ALU.mult))
            V.tensor_tensor(gate_of[:, 1:NE + 1, :].rearrange("p r c -> p c r"), first[:, :, :], second[:, :, :], ALU.add)
            chain(V.tensor_tensor(eq[:, 0:NE, :], low, over[:, :].unsqueeze(1).broadcast_to([P, NE, NE]), ALU.mult))
            chain(V.tensor_reduce(kx[:, :], eq[:, 0:NE, :], AX, ALU.add))
            for j in range(MORE):
                last = V.scalar_tensor_tensor(mj[:, j, :], kx[:, :], float(j), over[:, :], ALU.is_equal, ALU.mult)
            last.then_inc(tables_ready, 1)
            dve.wait_ge(route_ready, 1)
            rounds = dve.value_load(info[0:1, 0:1], min_val=NE, max_val=ROUNDS)
            with dve.Fori(0, rounds) as rnd:
                for n in range(U_EXP):
                    dve.wait_ge(hi_ready, rnd * U_EXP + (U_DENSE + n + 1))
                    V.tensor_tensor(wlo[:, n % SPLIT, :], raw[:, (U_DENSE + n) % RAW, :], whi[:, n % SPLIT, :].bitcast(F32), ALU.subtract).then_inc(lo_ready, 1)
                    if n == 1:
                        result_out(rnd)
                    for j in range(JB):
                        if n == UP_END(j) + 2:
                            dve.wait_ge(sg_ready_m, rnd * JB + (j + 1))
                            dve.wait_ge(multiplied, rnd * U_EXP + (U_DENSE + UP_END(j) + 1))
                            V.tensor_tensor(hid[:, j % 2, :], sg[:, j % 2, :], B[3 + 2 * (j % 2)][:, :], ALU.mult).then_inc(hid_ready_m, 1)
                        if n == HT_AT(j):
                            dve.wait_ge(ht_hi_ready, rnd * JB + (j + 1))
                            V.tensor_tensor(ht_lo[:, j % 2, :, :], B[6][:, :].rearrange("p (f s) -> p f s", f=4),
                                            ht_hi[:, j % 2, :, :].bitcast(F32), ALU.subtract).then_inc(ht_ready, 1)
                    if n == UP_END(0) + 2:
                        add_back(rnd)
                    if n == UP_END(JB - 1):
                        dve.wait_ge(placeT_done, rnd + 1)
                        dve.wait_ge(later_ready, 1)
                        picks(rnd + 1)
                packed_out(rnd + 1)
            result_out(rounds)
            add_back(rounds)
            dve.wait_ge(g_final_in, 16)
            for c in range(TC):
                rstd_of(4, c)
                V.scalar_tensor_tensor(xn[:, c, :], x[:, c, :], rstd[:, 4, c:c + 1], g_final[:, :], ALU.mult, ALU.mult).then_inc(final_ready, 1)


def kernel(**inputs):
    from concourse import bacc
    from concourse.bass_utils import run_bass_kernel_spmd

    a = {k: np.asarray(v) for k, v in inputs.items()}

    def column(v):
        return v.reshape(-1, P).T

    params = np.concatenate([
        column(a["ev_norm_mix"][0]), column(a["ev_norm_ffn"][0]), column(a["od_norm_mix"][0]), column(a["od_norm_ffn"][0]),
        a["ev_pool_scale"][0].T, column(a["ev_q_norm"][0]), column(a["ev_kv_norm"][0]),
        a["od_router"][0].reshape(KD, P, NE).transpose(1, 0, 2).reshape(P, -1),
        a["ev_pool_w"][0].transpose(1, 0, 2).reshape(P, -1),
        a["od_sgu_w"][0].transpose(2, 0, 1).reshape(P, -1)], axis=1)
    rows = np.concatenate([a["od_sgu_b"][0].reshape(-1), a["od_sgu_norm_g"][0].reshape(-1), a["od_sgu_norm_b"][0].reshape(-1)])
    offset = np.clip(np.arange(SEQ)[:, None] - np.arange(SEQ)[None, :], -REL, REL) + REL
    bias = a["od_rel_bias"][0][:, offset].transpose(1, 0, 2)
    arrays = {"x": a["x"], "consts": constants(), "params": params, "rows": rows, "g_ffn1": a["od_norm_ffn"][0], "g_final": a["final_norm"], "bias0": bias[0:P, :, 0:P], "bias1": bias[P:SEQ]}
    for name in ("ev_w_in", "ev_w_q_up", "ev_w_kv_up", "ev_w_out", "ev_ffn_w_gate", "ev_ffn_w_up", "ev_ffn_w_down", "od_w_in", "od_w_out",
                 "od_moe_w_gate", "od_moe_w_up", "od_moe_w_down"):
        arrays[name] = a[name][0]
    nc = bacc.Bacc("TRN2", target_bir_lowering=False, num_devices=1)
    feeds, t = {}, {}
    for name, v in arrays.items():
        v = np.ascontiguousarray(v)
        feeds[f"in_{name}"] = v
        t[name] = nc.dram_tensor(f"in_{name}", v.shape, mybir.dt.from_np(v.dtype), kind="ExternalInput").ap()
    t["out"] = nc.dram_tensor("out_0", (1, SEQ, D), F32, kind="ExternalOutput").ap()
    build(nc, t)
    r = run_bass_kernel_spmd(nc, [feeds], core_ids=[0])
    return r.results[0]["out_0"]
```

```python
from contextlib import ExitStack

import numpy as np
import concourse.bass as bass
from concourse import mybir

F32 = mybir.dt.float32
F32R = mybir.dt.float32r
I32 = mybir.dt.int32
ALU = mybir.AluOpType
ACT = mybir.ActivationFunctionType
AX = mybir.AxisListType.X

P = 128
D = 1024
KD = D // P
SEQ = 256
TC = SEQ // P
HEADS = 8
EPS = 1e-6
NEG = -1e30

POOL_G, POOL_W = 4, (2, 4, 8, 16)
PAD = 16
A_W = 512
QR, KVR, ROPE = 256, 128, 32
LAT = QR + KVR + ROPE
NOPE, VD, DQ = 64, 64, 96
HR = ROPE // 2
FF = 2816
HD = 64
REL = 128
NE = 8
EFF = 3584

UNIT = 2048
RAW = 6
RAW_E = 7
SPLIT = 3
SPLIT_D = 2
FFS = FF // 256
U_EVEN = 2 + 2 + 4
U_FFN = 3 * FFS
U_ODD = 10 + 4
U_DENSE = U_EVEN + U_FFN + U_ODD
JB = EFF // 512
U_EXP = 6 * JB
MORE = 3
ROUNDS = NE + MORE
assert U_EXP % RAW_E == 0 and U_EXP % SPLIT == 0

CONSTS = {}
_at = 0
for _n, _w in (("ident", P), ("tri", P), ("ones", P), ("causal", P), ("slot", P), ("mask0", P), ("mask1", 2 * P),
               ("cos", TC * HR), ("sin", TC * HR), ("invcnt", POOL_G * PAD), ("low", NE * NE), ("eidx", NE)):
    CONSTS[_n] = (_at, _at + _w)
    _at += _w
N_CONST = _at
PARAMS = {}
_at = 0
for _n, _w in (("g_mix0", KD), ("g_ffn0", KD), ("g_mix1", KD), ("g_ffn1", KD), ("pool_scale", POOL_G), ("q_norm", 2),
               ("kv_norm", 1), ("router", KD * NE), ("pool_w", POOL_G * P), ("sgu_w", POOL_G * P)):
    PARAMS[_n] = (_at, _at + _w)
    _at += _w
N_PARAM = _at
ROWS = {}
_at = 0
for _n, _w in (("sgu_b", 512), ("sgu_g", 512), ("sgu_nb", 512)):
    ROWS[_n] = (_at, _at + _w)
    _at += _w
N_ROW = _at


U_ODD0 = U_EVEN + U_FFN
PT_TILES = [(0, h, 0) for h in range(HEADS)] + [(1, h, kc) for h in range(HEADS) for kc in range(2)]
PT_BANK = (4, 5, 7, 4, 5, 7)


def FFN_GATE(step):
    return U_EVEN + (0 if step == 0 else 3 * step - 1)


def UP_END(j):
    return 3 if j == 0 else 6 * j + 1


def HT_AT(j):
    return 6 * j + 7 if j < JB - 1 else U_EXP - 2



def constants():
    c = np.zeros((P, N_CONST), np.float32)

    def put(name, value):
        a, b = CONSTS[name]
        c[:, a:b] = np.asarray(value, np.float32).reshape(P, b - a) if np.ndim(value) else value

    p, r = np.arange(P)[:, None], np.arange(P)[None, :]
    put("ident", p == r)
    put("tri", p < r)
    put("ones", 1.0)
    put("causal", p <= r)
    put("slot", np.broadcast_to(r + 1, (P, P)))
    keys = np.arange(2 * P)[None, :]
    put("mask0", np.where(r // 64 <= p // 64, 0.0, NEG))
    put("mask1", np.where(keys // 64 <= (P + p) // 64, 0.0, NEG))
    inv = (np.float32(1.0) / np.power(np.float32(10000.0), np.arange(0, ROPE, 2, dtype=np.float32) / np.float32(ROPE))).astype(np.float32)
    ang = (np.arange(SEQ, dtype=np.float32)[:, None] * inv[None, :]).astype(np.float32).astype(np.float64)
    put("cos", np.cos(ang).reshape(TC, P, HR).transpose(1, 0, 2).reshape(P, -1))
    put("sin", np.sin(ang).reshape(TC, P, HR).transpose(1, 0, 2).reshape(P, -1))
    t = np.arange(PAD)
    put("invcnt", np.broadcast_to(np.stack([1.0 / np.minimum(t + 1, w) for w in POOL_W]).reshape(1, -1), (P, POOL_G * PAD)))
    e = np.arange(NE)
    put("low", np.broadcast_to((e[None, :] < e[:, None]).reshape(1, -1), (P, NE * NE)))
    put("eidx", np.broadcast_to(e[None, :], (P, NE)))
    return c


def build(nc, t):
    ctx = ExitStack()
    with ctx:
        def sb(stack, name, shape, dt=F32):
            return stack.enter_context(nc.sbuf_tensor(name, shape, dt))

        def sem(name):
            return ctx.enter_context(nc.semaphore(name))

        raw = sb(ctx, "raw", [P, RAW, UNIT])
        cst = sb(ctx, "cst", [P, N_CONST])
        prm = sb(ctx, "prm", [P, N_PARAM])
        g_row = sb(ctx, "g_row", [P, D])
        x = sb(ctx, "x", [P, TC, D])
        ms = sb(ctx, "ms", [P, 5, TC, 2])
        mse = sb(ctx, "mse", [P, 5, TC])
        std = sb(ctx, "std", [P, 5, TC])
        rstd = sb(ctx, "rstd", [P, 5, TC])
        warm = sb(ctx, "warm", [P, 2])
        lms = sb(ctx, "lms", [P, 2, TC])
        lmse = sb(ctx, "lmse", [P, 2, TC])
        lstd = sb(ctx, "lstd", [P, 2, TC])
        lrstd = sb(ctx, "lrstd", [P, 2, TC])
        gmean = sb(ctx, "gmean", [P, TC * POOL_G])
        gvar = sb(ctx, "gvar", [P, TC * POOL_G])
        gstd = sb(ctx, "gstd", [P, TC * POOL_G])
        grs = sb(ctx, "grs", [P, TC * POOL_G])
        mx = sb(ctx, "mx", [P, TC, HEADS])
        nmx = sb(ctx, "nmx", [P, TC, HEADS])
        sums = sb(ctx, "sums", [P, TC, HEADS])
        rec = sb(ctx, "rec", [P, TC, HEADS])
        lg = sb(ctx, "lg", [P, TC, NE])
        gt = sb(ctx, "gt", [P, TC * NE, NE])
        eq = sb(ctx, "eq", [P, TC * NE, NE])
        rank = sb(ctx, "rank", [P, TC, NE])
        chosen = sb(ctx, "chosen", [P, TC, NE])
        first = sb(ctx, "first", [P, TC, NE])
        second = sb(ctx, "second", [P, TC, NE])
        v1 = sb(ctx, "v1", [P, TC])
        v2 = sb(ctx, "v2", [P, TC])
        dv = sb(ctx, "dv", [P, TC])
        ev = sb(ctx, "ev", [P, TC])
        w1 = sb(ctx, "w1", [P, TC])
        w2 = sb(ctx, "w2", [P, TC])
        tmp8 = sb(ctx, "tmp8", [P, TC, NE])
        over = sb(ctx, "over", [P, NE])
        kx = sb(ctx, "kx", [P, NE])
        mj = sb(ctx, "mj", [P, MORE, NE])
        fold = sb(ctx, "fold", [P, TC, NE])
        info_f = sb(ctx, "info_f", [P, 1 + MORE])
        info = sb(ctx, "info", [P, 1 + MORE], I32)
        slot_of = sb(ctx, "slot_of", [P, ROUNDS + 1, TC])
        gate_of = sb(ctx, "gate_of", [P, ROUNDS + 1, TC])
        A_RING, A_QK, A_S, A_MIX, A_H, A_X = 0, 8192, 12288, 15360, 19456, 23552
        A_E = 25600
        A_END = A_E + 7680
        arena_base = nc.sbuf_base
        arena = sb(ctx, "arena", [P, A_END])
        assert arena_base % 32 == 0 and arena.name

        def at(name, shape, start, dt=F32):
            size = int(np.prod(shape[1:]))
            assert start % 8 == 0 and start + size <= A_END, name
            return nc.alloc_sbuf_tensor_at(name, shape, dt, offset=arena_base + 4 * start)

        dw_hi = at("dw_hi", [P, SPLIT_D, UNIT], A_RING, F32R)
        dw_lo = at("dw_lo", [P, SPLIT_D, UNIT], A_RING + SPLIT_D * UNIT, F32R)
        qT = at("qT", [P, HEADS, SEQ], A_QK)
        kT = at("kT", [P, HEADS, SEQ], A_QK + 2048)
        S0 = at("S0", [P, HEADS, P], A_S)
        S1 = at("S1", [P, HEADS, SEQ], A_S + 1024)
        mix_hi = at("mix_hi", [P, KD, SEQ], A_MIX, F32R)
        mix_lo = at("mix_lo", [P, KD, SEQ], A_MIX + 2048, F32R)
        hT_hi = at("hT_hi", [P, KD, SEQ], A_H, F32R)
        hT_lo = at("hT_lo", [P, KD, SEQ], A_H + 2048, F32R)
        PT = at("PT", [P, 3 * HEADS, P], A_H)
        raw_more = at("raw_more", [P, UNIT], A_H + 2048)
        hT = at("hT", [P, KD, SEQ], A_H)
        xn = at("xn", [P, TC, D], A_X)
        vv = at("vv", [P, TC, HEADS * VD], A_X)
        att = at("att", [P, TC, HEADS * VD], A_X + 1024)
        lat = at("lat", [P, TC, LAT], A_S)
        latn = at("latn", [P, TC, QR + KVR], A_S + 832)
        kr96 = at("kr96", [P, TC, DQ], A_S + 1600)
        ropek = at("ropek", [P, 4, TC, HR], A_S + 1792)
        latT = at("latT", [P, 3, SEQ], A_S + 1920)
        qq = at("qq", [P, TC, HEADS, DQ], A_S + 2688)
        ropeq = at("ropeq", [P, 4, TC * HEADS, HR], A_S + 4224)
        apad = at("apad", [P, POOL_G, PAD + SEQ], A_E)
        win1 = at("win1", [P, POOL_G, PAD + SEQ], A_E + 1088)
        win2 = at("win2", [P, POOL_G, PAD + SEQ], A_E + 2176)
        pooled = at("pooled", [P, POOL_G, SEQ], A_E + 3264)
        early = at("early", [P, POOL_G, PAD], A_E + 4288)
        wq_up = at("wq_up", [P, 2, HEADS * DQ], A_E + 4352)
        wkv_up = at("wkv_up", [P, HEADS * (NOPE + VD)], A_E + 5888)
        silu0 = at("silu0", [P, 2, 2 * SEQ], A_QK)
        hid0 = at("hid0", [P, 2, 2 * SEQ], A_QK + 1024)
        hid_hi = at("hid_hi", [P, 2, 2 * SEQ], A_QK + 2048, F32R)
        hid_lo = at("hid_lo", [P, 2, 2 * SEQ], A_QK + 3072, F32R)
        bias0 = at("bias0", [P, HEADS, P], A_E)
        bias1 = at("bias1", [P, HEADS, SEQ], A_E + 1024)
        rows = at("rows", [P, N_ROW], A_E + 3072)
        gv = at("gv", [P, TC * POOL_G, P], A_E + 4608)
        gsq = at("gsq", [P, TC * POOL_G, P], A_E + 5632)
        mixed = at("mixed", [P, POOL_G, SEQ], A_E + 5632)
        uT = at("uT", [P, POOL_G, SEQ], A_E + 6656)
        whi = at("whi", [P, SPLIT, UNIT], A_RING, F32R)
        wlo = at("wlo", [P, SPLIT, UNIT], A_RING + SPLIT * UNIT, F32R)
        y_hi = at("y_hi", [P, D], A_S, F32R)
        y_lo = at("y_lo", [P, D], A_S + 1024, F32R)
        pick = at("pick", [P, TC, P], A_S + 2048)
        pickr = at("pickr", [P, TC, P], A_S + 2304, F32R)
        place = at("place", [P, TC, P], A_S + 2560, F32R)
        h_hi = at("h_hi", [P, TC, D], A_MIX, F32R)
        h_lo = at("h_lo", [P, TC, D], A_MIX + 2048, F32R)
        xe_hi = at("xe_hi", [P, KD, P], A_E, F32R)
        xe_lo = at("xe_lo", [P, KD, P], A_E + 1024, F32R)
        sg = at("sg", [P, 2, 512], A_E + 2048)
        hid = at("hid", [P, 2, 512], A_E + 3072)
        ht_hi = at("ht_hi", [P, 2, 4, P], A_E + 4096, F32R)
        ht_lo = at("ht_lo", [P, 2, 4, P], A_E + 5120, F32R)
        g_final = at("g_final", [P, D], A_E + 6144)
        B = [ctx.enter_context(nc.psum_tensor(f"bank{i}", [P, 512], F32)) for i in range(8)]

        def turned(layer, c, k):
            return B[(0 if layer == 0 else 4) + 2 * c + k // 4][:, (k % 4) * P:(k % 4 + 1) * P]

        def C(name):
            a, b = CONSTS[name]
            return cst[:, a:b]

        def PR(name):
            a, b = PARAMS[name]
            return prm[:, a:b]

        def RW(name):
            a, b = ROWS[name]
            return rows[:, a:b]

        ident_in, consts_in, params_in, rows_in = sem("ident_in"), sem("consts_in"), sem("params_in"), sem("rows_in")
        x_in = [sem(f"x_in{c}") for c in range(TC)]
        bias_in = sem("bias_in")
        raw_in = [sem(f"raw_in{s}") for s in range(RAW + 1)]
        multiplied = sem("multiplied")
        x_ready = sem("x_ready")
        sq_done, mse_ready, std_ready, warm_ready = sem("sq_done"), sem("mse_ready"), sem("std_ready"), sem("warm_ready")
        xn_ready, xT_done = sem("xn_ready"), sem("xT_done")
        hT_act, hT_dve = sem("hT_act"), sem("hT_dve")
        c0_done = sem("c0_done")
        dchain, achain = sem("dchain"), sem("achain")
        lat_copied, lsq_done, lmse_ready, lstd_ready = (sem("lat_copied"), sem("lsq_done"), sem("lmse_ready"), sem("lstd_ready"))
        latn_ready, latT_done, latT_ready, kr_ready = sem("latn_ready"), sem("latT_done"), sem("latT_ready"), sem("kr_ready")
        a_padded, pads_zeroed, win_ready = sem("a_padded"), sem("pads_zeroed"), sem("win_ready")
        pooled_ready, pool_done, pool_mixed = sem("pooled_ready"), sem("pool_done"), sem("pool_mixed")
        q_done, q_copied, q_ready, qT_done, qT_ready, qT_act = sem("q_done"), sem("q_copied"), sem("q_ready"), sem("qT_done"), sem("qT_ready"), sem("qT_act")
        v_done, v_ready, k_done, k_ready = sem("v_done"), sem("v_ready"), sem("k_done"), sem("k_ready")
        kr96_zeroed, up_in, pool_hi = sem("kr96_zeroed"), sem("up_in"), sem("pool_hi")
        s_done, s_read, mx_ready, exp_done, pt_done, pt_act, pt_dve = (sem("s_done"), sem("s_read"), sem("mx_ready"), sem("exp_done"), sem("pt_done"), sem("pt_act"), sem("pt_dve"))
        pv_done, att_ready, attT_done, attT_hi, attT_ready = sem("pv_done"), sem("att_ready"), sem("attT_done"), sem("attT_hi"), sem("attT_ready")
        silu_ready, hid_made, hid_hi_ready, hid_ready = sem("silu_ready"), sem("hid_made"), sem("hid_hi_ready"), sem("hid_ready")
        bias_ready, qz_zeroed, oq_ready, ok_ready = sem("bias_ready"), sem("qz_zeroed"), sem("oq_ready"), sem("ok_ready")
        ov_ready, gelu_gv, gelu_u, mixed_read = sem("ov_ready"), sem("gelu_gv"), sem("gelu_u"), sem("mixed_read")
        gvar_ready, gstd_ready, vn_ready, wsT_ready, mixed_done, sg_made, sg_hi_ready, sg_ready = (sem("gvar_ready"), sem("gstd_ready"), sem("vn_ready"), sem("wsT_ready"), sem("mixed_done"), sem("sg_made"), sem("sg_hi_ready"), sem("sg_ready"))
        logits_done, dv_ready, ev_ready, chosen_ready, slots_ready, pos_done = sem("logits_done"), sem("dv_ready"), sem("ev_ready"), sem("chosen_ready"), sem("slots_ready"), sem("pos_done")
        route_ready, later_ready, tables_ready, rchain = sem("route_ready"), sem("later_ready"), sem("tables_ready"), sem("rchain")
        g_row_in, g_final_in = sem("g_row_in"), sem("g_final_in")
        hi_ready, lo_ready, hg_ready = sem("hi_ready"), sem("lo_ready"), sem("hg_ready")
        pick_ready, gathered, xe_hi_ready, xe_ready = sem("pick_ready"), sem("gathered"), sem("xe_hi_ready"), sem("xe_ready")
        placeT_done, place_ready = sem("placeT_done"), sem("place_ready")
        sg_ready_m, hid_ready_m = sem("moe_silu_ready"), sem("moe_hid_ready")
        hT_done_m, ht_hi_ready, ht_ready = sem("moe_hidT_done"), sem("ht_hi_ready"), sem("ht_ready")
        y_hi_ready, y_ready = sem("y_hi_ready"), sem("y_ready")
        h_hi_ready, h_lo_ready = sem("h_hi_ready"), sem("h_lo_ready")
        scattered, added = sem("scattered"), sem("added")
        final_ready, out_done = sem("final_ready"), sem("out_done")

        def unit_width(n):
            return dense_units[n].shape[1] * dense_units[n].shape[2]

        def rows_of(w, r0, nk, c0, c1):
            return w[r0:r0 + nk * P, c0:c1].rearrange("(k p) n -> p k n", p=P)

        dense_units = []
        w_in0, w_in1 = t["ev_w_in"], t["od_w_in"]
        for half in range(2):
            dense_units.append(rows_of(w_in0, half * 512, 4, A_W, A_W + LAT))
        for c in range(2):
            dense_units.append(rows_of(w_in0, 0, KD, c * 256, c * 256 + 256))
        for c in range(4):
            dense_units.append(rows_of(t["ev_w_out"], c * 256, 2, 0, D))
        for step in range(FFS + 1):
            if step < FFS:
                dense_units.append(rows_of(t["ev_ffn_w_gate"], 0, KD, step * 256, step * 256 + 256))
                dense_units.append(rows_of(t["ev_ffn_w_up"], 0, KD, step * 256, step * 256 + 256))
            if step:
                dense_units.append(rows_of(t["ev_ffn_w_down"], (step - 1) * 256, 2, 0, D))
        for part in (4, 2):
            for half in range(2):
                dense_units.append(rows_of(w_in1, half * 512, 4, part * 512, part * 512 + 512))
        for c in range(4):
            dense_units.append(rows_of(w_in1, 0, KD, c * 256, c * 256 + 256))
        for c in range(2):
            dense_units.append(rows_of(w_in1, 0, KD, 1536 + c * 256, 1536 + c * 256 + 256))
        for c in (2, 3, 0, 1):
            dense_units.append(rows_of(t["od_w_out"], c * 256, 2, 0, D))
        assert len(dense_units) == U_DENSE

        def expert_unit(kind, e, j, half):
            w = t["od_moe_w_" + kind]
            if kind == "down":
                r0 = j * 512 + half * 256
                return w[bass.ds(e, 1), r0:r0 + 256, :].rearrange("e (k p) n -> p (e k) n", p=P)
            return w[bass.ds(e, 1), half * 512:half * 512 + 512, j * 512:j * 512 + 512].rearrange("e (k p) n -> p (e k) n", p=P)

        order = []
        for j in range(JB):
            order += [("gate", j, 0), ("gate", j, 1), ("up", j, 0), ("up", j, 1)]
            if j:
                order += [("down", j - 1, 0), ("down", j - 1, 1)]
        order += [("down", JB - 1, 0), ("down", JB - 1, 1)]
        assert len(order) == U_EXP

        def expert_slot(n):
            return RAW if n % RAW_E == 0 else (U_DENSE + n % RAW_E - 1) % RAW

        def raw_of(unit):
            if unit < U_DENSE:
                return raw[:, unit % RAW, :]
            slot = expert_slot(unit - U_DENSE)
            return raw_more[:, :] if slot == RAW else raw[:, slot, :]

        def landed(unit, rnd=0):
            if unit < U_DENSE:
                return raw_in[unit % RAW], 16 * (unit // RAW + 1)
            slot = expert_slot(unit - U_DENSE)
            before = len(range(slot, U_DENSE, RAW)) if slot < RAW else 0
            return raw_in[slot], 16 * (before + (unit - U_DENSE) // RAW_E + 1) + 16 * (U_EXP // RAW_E) * rnd

        block = ctx.enter_context(nc.Block())

        @block.sync
        def _(sp):
            x_dram = t["x"].rearrange("b (c p) d -> p (b c) d", p=P)
            sp.dma_start(x[:, 0, :], x_dram[:, 0, :]).then_inc(x_in[0], 16)
            sp.dma_start(x[:, 1, :], x_dram[:, 1, :]).then_inc(x_in[1], 16)
            sp.dma_start(cst[:, 0:P], t["consts"][:, 0:P]).then_inc(ident_in, 16)
            for n, src in enumerate(dense_units):
                if n >= RAW:
                    sp.wait_ge(lo_ready, n - RAW + 1)
                k, w = src.shape[1], src.shape[2]
                dst = raw[:, n % RAW, 0:k * w].rearrange("p (k n) -> p k n", k=k)
                sp.dma_start(dst, src).then_inc(raw_in[n % RAW], 16)
                if n == 0:
                    sp.dma_start(prm[:, :], t["params"]).then_inc(params_in, 16)
                if n == 1:
                    sp.dma_start(cst[:, P:], t["consts"][:, P:]).then_inc(consts_in, 16)
                if n == 3:
                    sp.dma_start(wq_up[:, :, :], t["ev_w_q_up"].rearrange("(k p) n -> p k n", p=P)).then_inc(up_in, 16)
                    sp.dma_start(wkv_up[:, :], t["ev_w_kv_up"]).then_inc(up_in, 16)
                    sp.dma_start(g_row[:, :], t["g_ffn1"].partition_broadcast(P)).then_inc(g_row_in, 16)
                if n == U_EVEN + 12:
                    sp.dma_start(bias0[:, :, :], t["bias0"]).then_inc(bias_in, 16)
                    sp.dma_start(bias1[:, :, :], t["bias1"]).then_inc(bias_in, 16)
                    sp.dma_start(rows[:, :], t["rows"].partition_broadcast(P)).then_inc(rows_in, 16)

            def expert(e, rnd):
                for n, (kind, j, half) in enumerate(order):
                    u = U_DENSE + n
                    sp.wait_ge(lo_ready, rnd * U_EXP + (u - RAW_E + 1))
                    src = expert_unit(kind, e, j, half)
                    dst = raw_of(u).rearrange("p (k n) -> p k n", k=src.shape[1])
                    sp.dma_start(dst, src).then_inc(landed(u)[0], 16)

            sp.wait_ge(pv_done, 2 * TC)
            sp.wait_ge(sg_ready, 1)
            sp.dma_start(g_final[:, :], t["g_final"].partition_broadcast(P)).then_inc(g_final_in, 16)
            with sp.Fori(0, NE) as e:
                expert(e, e)
            sp.wait_ge(later_ready, 1)
            rounds = sp.value_load(info[0:1, 0:1], min_val=NE, max_val=ROUNDS)
            with sp.If(rounds > NE):
                with sp.Fori(NE, rounds) as rnd:
                    e = sp.value_load(info[0:1, bass.ds(rnd - (NE - 1), 1)], min_val=0, max_val=NE - 1)
                    expert(e, rnd)
            with sp.Else():
                sp.nop()
            for n in range(SPLIT):
                sp.wait_ge(lo_ready, rounds * U_EXP + (U_DENSE + n - RAW_E + 1))
                sp.dma_start(raw_of(U_DENSE + n)[:, 0:P], t["consts"][:, 0:P]).then_inc(landed(U_DENSE + n)[0], 16)
            out = t["out"].rearrange("b (c p) d -> p (b c) d", p=P)
            for n in range(2 * TC):
                sp.wait_ge(final_ready, n + 1)
                c, cols = n // 2, slice((n % 2) * 512, (n % 2 + 1) * 512)
                sp.dma_start(out[:, c, cols], xn[:, c, cols]).then_inc(out_done, 16)
            sp.wait_ge(out_done, 16 * 2 * TC)

        @block.gpsimd
        def _(pool):
            pool.memset(warm[:, :], 1.0).then_inc(warm_ready, 1)
            pool.memset(kr96[:, :, 0:NOPE], 0.0).then_inc(kr96_zeroed, 1)
            pool.memset(apad[:, :, 0:PAD], 0.0).then_inc(pads_zeroed, 1)
            pool.wait_ge(a_padded, 2)
            pool.wait_ge(pads_zeroed, 1)
            src, n = apad, PAD + SEQ
            for step in range(POOL_G):
                sh = 1 << step
                lo = 2 * sh - 1
                dst = (win1, win2)[step % 2]
                if step:
                    pool.wait_ge(win_ready, step)
                pool.tensor_tensor(dst[:, step:, lo:n], src[:, step:, lo:n], src[:, step:, lo - sh:n - sh], ALU.add).then_inc(win_ready, 1)
                src = dst
            pool.wait_ge(params_in, 16)
            pool.wait_ge(consts_in, 16)
            wsT = PR("sgu_w").rearrange("p (g t) -> p g t", g=POOL_G)
            pool.tensor_tensor(wsT, wsT, C("causal").unsqueeze(1).broadcast_to([P, POOL_G, P]), ALU.mult).then_inc(wsT_ready, 1)

            def low_half_of(unit):
                pool.wait_ge(lo_ready, unit)
                pool.wait_ge(hi_ready, unit + 1)
                if unit < U_DENSE:
                    w, lo, hi = unit_width(unit), dw_lo[:, unit % SPLIT_D, :], dw_hi[:, unit % SPLIT_D, :]
                else:
                    w, lo, hi = UNIT, wlo[:, unit - U_DENSE, :], whi[:, unit - U_DENSE, :]
                pool.tensor_tensor(lo[:, 0:w], raw_of(unit)[:, 0:w], hi[:, 0:w].bitcast(F32), ALU.subtract).then_inc(lo_ready, 1)

            low_half_of(U_EVEN)
            pool.wait_ge(bias_in, 32)
            pool.tensor_tensor(bias0[:, :, :], bias0[:, :, :], C("mask0").unsqueeze(1).broadcast_to([P, HEADS, P]), ALU.add).then_inc(bias_ready, 1)
            pool.tensor_tensor(bias1[:, :, :], bias1[:, :, :], C("mask1").unsqueeze(1).broadcast_to([P, HEADS, SEQ]), ALU.add).then_inc(bias_ready, 1)
            low_half_of(U_ODD0)
            pool.wait_ge(multiplied, U_ODD0)
            pool.memset(qT[:, :, :], 0.0).then_inc(qz_zeroed, 1)
            pool.wait_ge(gelu_u, 2)
            pool.wait_ge(mixed_read, 2)
            pool.tensor_tensor(mixed[:, :, :], mixed[:, :, :], uT[:, :, :], ALU.mult).then_inc(sg_made, 1)
            pool.wait_ge(sg_hi_ready, 1)
            pool.tensor_tensor(mix_lo[:, 4:8, :], mixed[:, :, :], mix_hi[:, 4:8, :].bitcast(F32), ALU.subtract).then_inc(sg_ready, 1)
            pool.wait_ge(g_row_in, 16)
            for c in range(TC):
                pool.wait_ge(xT_done, 2 * (3 * TC + c + 1))
                pool.tensor_tensor(xn[:, c, :], xn[:, c, :], g_row[:, :], ALU.mult).then_inc(hg_ready, 1)
            pool.memset(place[:, :, :].bitcast(F32), 0.0).then_inc(place_ready, 1)
            pool.memset(y_hi[:, :].bitcast(F32), 0.0).then_inc(y_ready, 1)
            pool.memset(y_lo[:, :].bitcast(F32), 0.0).then_inc(y_ready, 1)
            low_half_of(U_DENSE + 1)
            steps = [0]

            def chain(ins):
                steps[0] += 1
                ins.then_inc(rchain, 1)
                pool.wait_ge(rchain, steps[0])

            def fold_into(out, buf):
                chain(pool.tensor_tensor(buf[:, :, 0:4], buf[:, :, 0:4], buf[:, :, 4:8], ALU.add))
                chain(pool.tensor_tensor(buf[:, :, 0:2], buf[:, :, 0:2], buf[:, :, 2:4], ALU.add))
                chain(pool.tensor_tensor(out, buf[:, :, 0], buf[:, :, 1], ALU.add))

            pool.wait_ge(tables_ready, 1)
            for j in range(MORE):
                mask = mj[:, j, :].unsqueeze(1).broadcast_to([P, TC, NE])
                chain(pool.tensor_tensor(fold[:, :, :], mask, slot_of[:, 0:NE, :].rearrange("p r c -> p c r"), ALU.mult))
                fold_into(slot_of[:, NE + j, :], fold)
                chain(pool.tensor_tensor(fold[:, :, :], mask, gate_of[:, 1:NE + 1, :].rearrange("p r c -> p c r"), ALU.mult))
                fold_into(gate_of[:, NE + 1 + j, :], fold)
                chain(pool.tensor_tensor(fold[:, 0:1, :], mj[:, j:j + 1, :], C("eidx").unsqueeze(1), ALU.mult))
                fold_into(info_f[:, 1 + j:2 + j], fold[:, 0:1, :])
            chain(pool.tensor_scalar(slot_of[:, NE:NE + MORE, :], slot_of[:, NE:NE + MORE, :], -float(P), None, ALU.add))
            pool.tensor_copy(info[:, 1:], info_f[:, 1:]).then_inc(later_ready, 1)

        @block.tensor
        def _(pe):
            mm, tr = nc.tensor.matmul, nc.tensor.transpose
            pe.wait_ge(ident_in, 16)
            ident = C("ident")
            unit_no = [0]

            def take(k, w):
                n = unit_no[0]
                unit_no[0] += 1
                pe.wait_ge(lo_ready, n + 1)
                return [v[:, n % SPLIT_D, 0:k * w].rearrange("p (k n) -> p k n", k=k) for v in (dw_hi, dw_lo)]

            def product(out, a, b, first, last):
                mm(out, a[0], b[0], start=first, stop=False)
                mm(out, a[0], b[1], start=False, stop=False)
                return mm(out, a[1], b[0], start=False, stop=last)

            def transpose_x(layer, c):
                for b in range(2):
                    pe.wait_ge(xn_ready, 2 * (TC * layer + c) + b + 1)
                    for k in range(4 * b, 4 * b + 4):
                        last = tr(turned(layer, c, k), xn[:, c, k * P:(k + 1) * P], ident)
                    last.then_inc(xT_done, 1)

            def tokens_major(layer, banks, width):
                for half in range(2):
                    w = take(4, width)
                    for c in range(TC):
                        for k in range(4):
                            kk = half * 4 + k
                            pe.wait_ge(hT_dve, TC * KD * layer + 4 * (TC * half + c) + k + 1)
                            last = product(banks[c][:, 0:width], [h[:, kk, c * P:(c + 1) * P] for h in (hT_hi, hT_lo)], [v[:, k, :] for v in w],
                                           kk == 0, kk == KD - 1)
                    last.then_inc(multiplied, 1)

            def features_major(layer, bank):
                w = take(KD, 256)
                for m in range(2):
                    for k in range(KD):
                        pe.wait_ge(hT_dve, TC * KD * layer + 4 * (TC * (k // 4) + 1) + k % 4 + 1)
                        last = product(bank[:, m * SEQ:(m + 1) * SEQ], [v[:, k, m * P:(m + 1) * P] for v in w], [h[:, k, :] for h in (hT_hi, hT_lo)],
                                       k == 0, k == KD - 1)
                last.then_inc(multiplied, 1)

            def to_width(w, c, chunk_of, first, last):
                for k in range(2):
                    for half in range(2):
                        ins = product(B[2 * c + half][:, :], chunk_of(k, c), [v[:, k, half * 512:(half + 1) * 512] for v in w],
                                      first and k == 0, last and k == 1)
                return ins

            def back_to_width(n, units, chunk_of):
                w = take(2, D)
                ins = to_width(w, 0, chunk_of, n == 0, n == units - 1)
                if n == units - 1:
                    ins.then_inc(c0_done, 1)
                to_width(w, 1, chunk_of, n == 0, n == units - 1).then_inc(multiplied, 1)

            def scores(c, q_of, k_of):
                for h in range(HEADS):
                    if c == 0:
                        out = B[4 + h // 4][:, (h % 4) * P:(h % 4 + 1) * P]
                    else:
                        out = B[h // 2][:, (h % 2) * SEQ:(h % 2 + 1) * SEQ]
                    last = mm(out, q_of(h)[:, c * P:(c + 1) * P], k_of(h)[:, 0:(c + 1) * P], start=True, stop=True)
                    if (h + 1) % (2 if c else 4) == 0:
                        last.then_inc(s_done, 1)

            def turn_probs(layer, b):
                pe.wait_ge(exp_done, 16 * layer + (4 * (b + 1) if b < 2 else 8 + 2 * (b - 1)))
                if b >= 3:
                    pe.wait_ge(*((pt_act, 3 * layer + 1) if b == 4 else (pt_dve, 3 * layer + (1 if b == 3 else 2))))
                for n, (c, h, kc) in enumerate(PT_TILES[4 * b:4 * b + 4]):
                    src = S0[:, h, :] if c == 0 else S1[:, h, kc * P:(kc + 1) * P]
                    last = tr(B[PT_BANK[b]][:, n * P:(n + 1) * P], src, ident)
                last.then_inc(pt_done, 1)

            def weigh_values(layer, c):
                pe.wait_ge(pt_act, 3 * layer + (1 if c == 0 else 3))
                pe.wait_ge(pt_dve, 3 * layer + (1 if c == 0 else 3))
                if c:
                    pe.wait_ge(att_ready, TC * layer + 1)
                for h in range(HEADS):
                    for kc in range(c + 1):
                        n = h if c == 0 else HEADS + 2 * h + kc
                        last = mm(B[6][:, h * VD:(h + 1) * VD], PT[:, n, :], vv[:, kc, h * VD:(h + 1) * VD], start=(kc == 0), stop=(kc == c))
                last.then_inc(pv_done, 1)

            def attend_and_project(layer, other0, att0, other_ready):
                def chunk_from(m0):
                    return lambda k, c: [v[:, m0 + k, c * P:(c + 1) * P] for v in (mix_hi, mix_lo)]

                turn_probs(layer, 0)
                turn_probs(layer, 1)
                pe.wait_ge(s_read, TC * (layer + 1))
                pe.wait_ge(*other_ready)
                back_to_width(0, 4, chunk_from(other0))
                weigh_values(layer, 0)
                for b in range(2, 6):
                    turn_probs(layer, b)
                weigh_values(layer, 1)
                w = take(2, D)
                to_width(w, 0, chunk_from(other0 + 2), False, False)
                for c in range(TC):
                    pe.wait_ge(att_ready, TC * layer + c + 1)
                    for m in range(4):
                        last = tr(B[4 + m // 2][:, (m % 2) * SEQ + c * P:(m % 2) * SEQ + c * P + P], att[:, c, m * P:(m + 1) * P], ident)
                last.then_inc(attT_done, 1)
                to_width(w, 1, chunk_from(other0 + 2), False, False).then_inc(multiplied, 1)
                pe.wait_ge(attT_ready, 2 * (layer + 1))
                back_to_width(2, 4, chunk_from(att0))
                back_to_width(3, 4, chunk_from(att0 + 2))

            transpose_x(0, 0)
            transpose_x(0, 1)
            tokens_major(0, (B[4], B[5]), LAT)
            features_major(0, B[6])
            features_major(0, B[7])
            pe.wait_ge(latn_ready, 3)
            pe.wait_ge(kr96_zeroed, 1)
            for c in range(TC):
                for m in range(2):
                    tr(B[0][:, m * SEQ + c * P:m * SEQ + c * P + P], latn[:, c, m * P:(m + 1) * P], ident)
                tr(B[1][:, c * P:(c + 1) * P], latn[:, c, QR:QR + KVR], ident)
                last = tr(B[1][0:DQ, SEQ + c * P:SEQ + (c + 1) * P], kr96[:, c, :], ident)
            last.then_inc(latT_done, 1)
            pe.wait_ge(latT_ready, 2)
            pe.wait_ge(up_in, 32)
            pe.wait_ge(lat_copied, 2)
            for c in range(TC):
                for half in range(2):
                    for k in range(2):
                        last = mm(B[2 + 2 * c + half][:, 0:4 * DQ], latT[:, k, c * P:(c + 1) * P], wq_up[:, k, half * 4 * DQ:(half + 1) * 4 * DQ],
                                  start=(k == 0), stop=(k == 1))
            last.then_inc(q_done, 1)
            wv = wkv_up[:, :].rearrange("p (h d) -> p h d", h=HEADS)
            pe.wait_ge(latT_ready, 3)
            pe.wait_ge(a_padded, 2)
            for c in range(TC):
                last = mm(B[6 + c][:, :].rearrange("p (h d) -> p h d", h=HEADS), latT[:, 2, c * P:(c + 1) * P], wv[:, :, NOPE:NOPE + VD], start=True, stop=True)
            last.then_inc(v_done, 1)
            pe.wait_ge(kr_ready, 1)
            for h in range(HEADS):
                if h == 4:
                    pe.wait_ge(q_copied, 4)
                last = mm(B[h // 2][0:NOPE, (h % 2) * SEQ:(h % 2 + 1) * SEQ], wv[:, h, 0:NOPE], latT[:, 2, :], start=True, stop=True)
                if h % 4 == 3:
                    last.then_inc(k_done, 1)
            pe.wait_ge(pooled_ready, 1)
            pe.wait_ge(v_ready, 2)
            pw = PR("pool_w").rearrange("p (g d) -> p g d", g=POOL_G)
            for g in range(POOL_G):
                last = mm(B[6 + g // 2][:, (g % 2) * SEQ:(g % 2 + 1) * SEQ], pw[:, g, :], pooled[:, g, :], start=True, stop=True)
            last.then_inc(pool_done, 1)
            pe.wait_ge(q_ready, 2)
            pe.wait_ge(k_ready, 4)
            for h in range(HEADS):
                for c in range(TC):
                    last = tr(B[h // 2][0:DQ, (h % 2) * SEQ + c * P:(h % 2) * SEQ + c * P + P], qq[:, c, h, :], ident)
                if h % 2:
                    last.then_inc(qT_done, 1)
            q_of, k_of = (lambda h: qT[0:DQ, h, :]), (lambda h: kT[0:DQ, h, :])
            pe.wait_ge(qT_ready, 2)
            pe.wait_ge(qT_act, 2)
            scores(0, q_of, k_of)
            scores(1, q_of, k_of)
            attend_and_project(0, 0, 4, (pool_mixed, 4))
            transpose_x(1, 0)
            transpose_x(1, 1)
            for step in range(FFS + 1):
                if step < FFS:
                    if step >= 2:
                        pe.wait_ge(hid_made, step - 1)
                    features_major(1, B[4 + 2 * (step % 2)])
                    features_major(1, B[5 + 2 * (step % 2)])
                if step:
                    pe.wait_ge(hid_ready, step)
                    b = (step - 1) % 2
                    back_to_width(step - 1, FFS, lambda k, c: [v[:, b, k * SEQ + c * P:k * SEQ + (c + 1) * P] for v in (hid_hi, hid_lo)])
            transpose_x(2, 0)
            transpose_x(2, 1)
            tokens_major(2, (B[0], B[1]), 512)
            tokens_major(2, (B[2], B[3]), 512)
            for c in range(4):
                features_major(2, B[4 + c])
            pe.wait_ge(vn_ready, 1)
            pe.wait_ge(wsT_ready, 1)
            pe.wait_ge(ov_ready, 2)
            wsT = PR("sgu_w").rearrange("p (g t) -> p g t", g=POOL_G)
            for g in range(POOL_G):
                for c in range(TC):
                    last = mm(B[2 + g // 2][:, (g % 2) * SEQ + c * P:(g % 2) * SEQ + c * P + P], gv[:, c * POOL_G + g, :], wsT[:, g, :], start=True, stop=True)
            last.then_inc(mixed_done, 1)
            pe.wait_ge(gelu_gv, 2)
            for c in range(2):
                features_major(2, B[c])
            q_of, k_of = (lambda h: qT[:, h, :]), (lambda h: kT[:, h // 2, :])
            pe.wait_ge(oq_ready, 4)
            pe.wait_ge(ok_ready, 2)
            scores(0, q_of, k_of)
            pe.wait_ge(gelu_u, 2)
            pe.wait_ge(mixed_read, 2)
            scores(1, q_of, k_of)
            attend_and_project(1, 4, 0, (sg_ready, 1))
            router = PR("router").rearrange("p (k e) -> p k e", k=KD)
            transpose_x(3, 0)
            transpose_x(3, 1)
            for c in range(TC):
                pe.wait_ge(hT_act, 3 * TC * KD + 4 * (c + 1))
                pe.wait_ge(hT_dve, 3 * TC * KD + 4 * (c + 1))
                for k in range(KD):
                    last = mm(B[0][:, c * NE:(c + 1) * NE], hT[:, k, c * P:(c + 1) * P], router[:, k, :], start=(k == 0), stop=(k == KD - 1))
            last.then_inc(logits_done, 1)
            pe.wait_ge(chosen_ready, 1)
            pe.wait_ge(consts_in, 16)
            tri, ones = C("tri"), C("ones")
            mm(B[1][:, 0:2 * NE].rearrange("p (c e) -> p c e", c=TC), tri, chosen[:, :, :], start=True, stop=False)
            mm(B[1][:, NE:2 * NE], ones, chosen[:, 0, :], start=False, stop=True)
            mm(B[1][:, 2 * NE:3 * NE], ones, chosen[:, 0, :], start=True, stop=False)
            mm(B[1][:, 2 * NE:3 * NE], ones, chosen[:, 1, :], start=False, stop=True).then_inc(pos_done, 1)
            def gather(rnd):
                pe.wait_ge(pick_ready, rnd * 4 + 4)
                for k in range(KD):
                    n = 0
                    for part in (h_hi, h_lo):
                        for c in range(TC):
                            last = mm(B[4 + k // 4][:, (k % 4) * P:(k % 4 + 1) * P], part[:, c, k * P:(k + 1) * P], pickr[:, c, :],
                                      start=(n == 0), stop=(n == 3))
                            n += 1
                    if k % 4 == 3:
                        last.then_inc(gathered, 1)

            def scatter(rnd):
                pe.wait_ge(y_ready, rnd * 2 + 2)
                pe.wait_ge(place_ready, rnd + 1)
                for c in range(TC):
                    for half in range(2):
                        mm(B[4 + 2 * c + half][:, :], place[:, c, :], y_hi[:, half * 512:(half + 1) * 512], start=True, stop=False)
                        mm(B[4 + 2 * c + half][:, :], place[:, c, :], y_lo[:, half * 512:(half + 1) * 512], start=False, stop=True).then_inc(scattered, 1)

            pe.wait_ge(h_hi_ready, 2)
            pe.wait_ge(h_lo_ready, 2)
            gather(0)
            pe.wait_ge(route_ready, 1)
            rounds = pe.value_load(info[0:1, 0:1], min_val=NE, max_val=ROUNDS)
            with pe.Fori(0, rounds) as rnd:
                def unit(n):
                    pe.wait_ge(lo_ready, rnd * U_EXP + (U_DENSE + n + 1))
                    u = n % SPLIT
                    return whi[:, u, :], wlo[:, u, :]

                def project(bank, n):
                    for half in range(2):
                        hi, lo = unit(n + half)
                        if n == 0:
                            pe.wait_ge(xe_ready, rnd * 2 + (half + 1))
                        for k in range(4):
                            kk = 4 * half + k
                            last = product(bank[:, :], (xe_hi[:, kk, :], xe_lo[:, kk, :]), (hi[:, k * 512:(k + 1) * 512], lo[:, k * 512:(k + 1) * 512]),
                                           kk == 0, kk == KD - 1)
                        last.then_inc(multiplied, 1)

                def project_down(j, n):
                    pe.wait_ge(ht_ready, rnd * JB + (j + 1))
                    for part in range(2):
                        hi, lo = unit(n + part)
                        for m in range(2):
                            f = 2 * part + m
                            for half in range(2):
                                a = m * D + half * 512
                                last = product(B[half][:, :], (ht_hi[:, j % 2, f, :], ht_lo[:, j % 2, f, :]), (hi[:, a:a + 512], lo[:, a:a + 512]),
                                               j == 0 and f == 0, j == JB - 1 and f == 3)
                        last.then_inc(multiplied, 1)

                def transpose_hidden(j):
                    pe.wait_ge(hid_ready_m, rnd * JB + (j + 1))
                    if j:
                        pe.wait_ge(ht_ready, rnd * JB + j)
                    for f in range(4):
                        last = tr(B[6][:, f * P:(f + 1) * P], hid[:, j % 2, f * P:(f + 1) * P], ident)
                    last.then_inc(hT_done_m, 1)

                n = 0
                for j in range(JB):
                    if j >= 2:
                        pe.wait_ge(hid_ready_m, rnd * JB + (j - 1))
                    project(B[2 + 2 * (j % 2)], n)
                    n += 2
                    if j:
                        transpose_hidden(j - 1)
                    else:
                        scatter(rnd)
                    project(B[3 + 2 * (j % 2)], n)
                    n += 2
                    if j == 0:
                        pe.wait_ge(added, rnd * 4 + 4)
                        for c in range(TC):
                            last = tr(B[7][:, c * P:(c + 1) * P], pick[:, c, :], ident)
                        last.then_inc(placeT_done, 1)
                    else:
                        if j == JB - 1:
                            gather(rnd + 1)
                            transpose_hidden(j)
                        project_down(j - 1, n)
                        n += 2
                project_down(JB - 1, n)
            scatter(rounds)

        @block.scalar
        def _(act):
            A = nc.scalar.activation
            steps = [0]

            def chain(ins):
                steps[0] += 1
                ins.then_inc(achain, 1)
                act.wait_ge(achain, steps[0])

            split_no = [0]

            def split_to(n):
                while split_no[0] <= n:
                    u = split_no[0]
                    split_no[0] += 1
                    s, v = landed(u)
                    act.wait_ge(s, v)
                    if SPLIT_D <= u < U_DENSE:
                        act.wait_ge(multiplied, u - SPLIT_D + 1)
                    if u >= U_DENSE:
                        act.wait_ge(multiplied, U_DENSE)
                        A(whi[:, u - U_DENSE, :], raw_of(u), ACT.Copy).then_inc(hi_ready, 1)
                        continue
                    w = unit_width(u)
                    A(dw_hi[:, u % SPLIT_D, 0:w], raw[:, u % RAW, 0:w], ACT.Copy).then_inc(hi_ready, 1)

            def load_table(func):
                act.wait_ge(warm_ready, 1)
                chain(A(warm[:, 1:2], warm[:, 0:1], func))

            def mean_square(layer, c, ready):
                for half in range(2):
                    act.wait_ge(*ready(c, half))
                    cols = slice(half * 512, (half + 1) * 512)
                    A(xn[:, c, cols], x[:, c, cols], ACT.Square, scale=D ** -0.5, accum_out=ms[:, layer, c, half:half + 1]).then_inc(sq_done, 1)
                act.wait_ge(sq_done, 2 * (TC * layer + c + 1))
                act.wait_ge(mse_ready, TC * layer + c + 1)
                A(std[:, layer, c:c + 1], ms[:, layer, c, 1:2], ACT.Sqrt, bias=mse[:, layer, c:c + 1]).then_inc(std_ready, 1)

            def residual(layer):
                return (lambda c, half: (x_in[c], 16)) if layer == 0 else (lambda c, half: (x_ready, 4 * (layer - 1) + 2 * c + half + 1))

            def norm(layer, gain, ahead, func):
                load_table(ACT.Sqrt)
                mean_square(layer, 0, residual(layer))
                mean_square(layer, 1, residual(layer))
                if layer == 0:
                    split_to(0)
                    act.wait_ge(params_in, 16)
                for b in range(2):
                    for c in range(TC):
                        act.wait_ge(xT_done, 2 * (TC * layer + c) + b + 1)
                        for k in range(4 * b, 4 * b + 4):
                            A(hT_hi[:, k, c * P:(c + 1) * P], turned(layer, c, k), ACT.Copy, scale=PR(gain)[:, k:k + 1]).then_inc(hT_act, 1)
                split_to(ahead)
                load_table(func)

            def softmax(layer, out0):
                for c in range(TC):
                    act.wait_ge(mx_ready, TC * layer + c + 1)
                    for h in range(HEADS):
                        s = S0[:, h, :] if c == 0 else S1[:, h, :]
                        A(s, s, ACT.Exp, bias=nmx[:, c, h:h + 1], accum_out=sums[:, c, h:h + 1]).then_inc(exp_done, 1)
                    if c == 0:
                        split_to(out0 + 1)
                        probs_out(layer, 1)
                probs_out(layer, 3)
                probs_out(layer, 5)

            def probs_out(layer, b):
                act.wait_ge(pt_done, 6 * layer + b + 1)
                A(PT[:, 4 * b:4 * b + 4, :], B[PT_BANK[b]][:, :].rearrange("p (n q) -> p n q", n=4), ACT.Copy).then_inc(pt_act, 1)

            def mix_out(layer, c0, out0):
                split_to(out0 + 2)
                act.wait_ge(attT_done, layer + 1)
                for b in range(2):
                    A(mix_hi[:, c0 + 2 * b:c0 + 2 * b + 2, :], B[4 + b][:, :].rearrange("p (m t) -> p m t", m=2), ACT.Copy).then_inc(attT_hi, 1)
                split_to(out0 + 3)

            norm(0, "g_mix0", 0, ACT.Sqrt)
            split_to(3)
            act.wait_ge(multiplied, 2)
            for c in range(TC):
                A(lat[:, c, :], B[4 + c][:, 0:LAT], ACT.Copy).then_inc(lat_copied, 1)
            act.wait_ge(lat_copied, 2)
            for c in range(TC):
                A(latn[:, c, 0:QR], lat[:, c, 0:QR], ACT.Square, scale=QR ** -0.5, accum_out=lms[:, 0, c:c + 1]).then_inc(lsq_done, 1)
                A(latn[:, c, QR:QR + KVR], lat[:, c, QR:QR + KVR], ACT.Square, scale=KVR ** -0.5, accum_out=lms[:, 1, c:c + 1]).then_inc(lsq_done, 1)
            act.wait_ge(lmse_ready, 1)
            A(lstd[:, :, :], lmse[:, :, :], ACT.Sqrt).then_inc(lstd_ready, 1)
            load_table(ACT.Exp)
            for b in range(2):
                act.wait_ge(multiplied, 3 + b)
                A(apad[:, 2 * b:2 * b + 2, PAD:], B[6 + b][:, :].rearrange("p (g t) -> p g t", g=2), ACT.Copy).then_inc(a_padded, 1)
                split_to(4 + b)
            act.wait_ge(q_done, 1)
            for c in range(TC):
                for half in range(2):
                    A(qq[:, c, half * 4:(half + 1) * 4, :], B[2 + 2 * c + half][:, 0:4 * DQ].rearrange("p (h d) -> p h d", h=4), ACT.Copy).then_inc(q_copied, 1)
            for b in range(4):
                act.wait_ge(k_done, 1 + b // 2)
                A(kT[0:NOPE, 2 * b:2 * b + 2, :], B[b][0:NOPE, :].rearrange("p (h t) -> p h t", h=2), ACT.Copy).then_inc(k_ready, 1)
            for b in (1, 3):
                act.wait_ge(qT_done, b + 1)
                A(qT[0:DQ, 2 * b:2 * b + 2, :], B[b][0:DQ, :].rearrange("p (h t) -> p h t", h=2), ACT.Copy).then_inc(qT_act, 1)
            act.wait_ge(pool_done, 1)
            for g in range(POOL_G):
                A(mix_hi[:, g, :], B[6 + g // 2][:, (g % 2) * SEQ:(g % 2 + 1) * SEQ], ACT.Copy, scale=PR("pool_scale")[:, g:g + 1]).then_inc(pool_hi, 1)
            softmax(0, 4)
            mix_out(0, 4, 4)
            split_to(U_EVEN)
            norm(1, "g_ffn0", U_EVEN + 1, ACT.Silu)
            for step in range(FFS):
                gate = FFN_GATE(step)
                split_to(gate + 1)
                act.wait_ge(multiplied, gate + 1)
                if step >= 2:
                    act.wait_ge(hid_made, step - 1)
                A(silu0[:, step % 2, :], B[4 + 2 * (step % 2)][:, :], ACT.Silu).then_inc(silu_ready, 1)
                split_to(gate + 3 if step else gate + 2)
                act.wait_ge(hid_made, step + 1)
                A(hid_hi[:, step % 2, :], hid0[:, step % 2, :], ACT.Copy).then_inc(hid_hi_ready, 1)
            split_to(U_ODD0)
            norm(2, "g_mix1", U_ODD0 + 1, ACT.Gelu_apprx_tanh)
            split_to(U_ODD0 + 2)
            act.wait_ge(multiplied, U_ODD0 + 2)
            for c in range(TC):
                A(gv[:, c * POOL_G:(c + 1) * POOL_G, :], B[c][:, :].rearrange("p (g d) -> p g d", g=POOL_G), ACT.Gelu_apprx_tanh).then_inc(gelu_gv, 1)
            split_to(U_ODD0 + 4)
            act.wait_ge(multiplied, U_ODD0 + 4)
            for c in range(TC):
                A(vv[:, c, :], B[2 + c][:, :], ACT.Copy).then_inc(ov_ready, 1)
            split_to(U_ODD0 + 5)
            act.wait_ge(gvar_ready, 1)
            A(gstd[:, :], gvar[:, :], ACT.Sqrt).then_inc(gstd_ready, 1)
            load_table(ACT.Gelu_apprx_tanh)
            split_to(U_ODD0 + 7)
            for b in range(2):
                act.wait_ge(multiplied, U_ODD0 + 7 + b)
                A(kT[:, 2 * b:2 * b + 2, :], B[6 + b][:, :].rearrange("p (m t) -> p m t", m=2), ACT.Copy).then_inc(ok_ready, 1)
                split_to(U_ODD0 + 8 + b)
            for b in range(2):
                act.wait_ge(multiplied, U_ODD0 + 9 + b)
                A(uT[:, 2 * b:2 * b + 2, :], B[b][:, :].rearrange("p (g t) -> p g t", g=2), ACT.Gelu_apprx_tanh).then_inc(gelu_u, 1)
                if b == 0:
                    split_to(U_ODD0 + 10)
            load_table(ACT.Exp)
            act.wait_ge(sg_made, 1)
            A(mix_hi[:, 4:8, :], mixed[:, :, :], ACT.Copy).then_inc(sg_hi_ready, 1)
            softmax(1, U_ODD0 + 10)
            mix_out(1, 0, U_ODD0 + 10)
            load_table(ACT.Sqrt)
            mean_square(3, 0, residual(3))
            mean_square(3, 1, residual(3))
            for c in range(TC):
                act.wait_ge(xT_done, 2 * (3 * TC + c) + 1)
                for k in range(4):
                    A(hT[:, k, c * P:(c + 1) * P], turned(3, c, k), ACT.Copy, scale=PR("g_ffn1")[:, k:k + 1]).then_inc(hT_act, 1)
            split_to(U_DENSE)
            for c in range(TC):
                act.wait_ge(hg_ready, c + 1)
                A(h_hi[:, c, :], xn[:, c, :], ACT.Copy).then_inc(h_hi_ready, 1)
            split_to(U_DENSE + SPLIT - 1)
            load_table(ACT.Exp)
            act.wait_ge(dv_ready, 1)
            A(ev[:, :], dv[:, :], ACT.Exp).then_inc(ev_ready, 1)
            load_table(ACT.Silu)
            act.wait_ge(route_ready, 1)
            rounds = act.value_load(info[0:1, 0:1], min_val=NE, max_val=ROUNDS)

            def packed_out(rnd):
                for b in range(2):
                    act.wait_ge(gathered, rnd * 2 + (b + 1))
                    A(xe_hi[:, 4 * b:4 * b + 4, :], B[4 + b][:, :].rearrange("p (k s) -> p k s", k=4), ACT.Copy).then_inc(xe_hi_ready, 1)

            def result_out():
                for half in range(2):
                    A(y_hi[:, half * 512:(half + 1) * 512], B[half][:, :], ACT.Copy).then_inc(y_hi_ready, 1)

            packed_out(0)
            with act.Fori(0, rounds) as rnd:
                for n in range(SPLIT, U_EXP + SPLIT):
                    act.wait_ge(*landed(U_DENSE + n, rnd))
                    act.wait_ge(multiplied, rnd * U_EXP + (U_DENSE + n - SPLIT + 1))
                    A(whi[:, n % SPLIT, :], raw_of(U_DENSE + n), ACT.Copy).then_inc(hi_ready, 1)
                    if n == U_EXP + 1:
                        act.wait_ge(multiplied, (rnd + 1) * U_EXP + U_DENSE)
                        result_out()
                    for j in range(JB):
                        if n == UP_END(j) + 2:
                            act.wait_ge(multiplied, rnd * U_EXP + (U_DENSE + UP_END(j) - 1))
                            if j >= 2:
                                act.wait_ge(hid_ready_m, rnd * JB + (j - 1))
                            A(sg[:, j % 2, :], B[2 + 2 * (j % 2)][:, :], ACT.Silu).then_inc(sg_ready_m, 1)
                        if n == HT_AT(j) and j == JB - 1:
                            packed_out(rnd + 1)
                        if n == HT_AT(j):
                            act.wait_ge(hT_done_m, rnd * JB + (j + 1))
                            A(ht_hi[:, j % 2, :, :], B[6][:, :].rearrange("p (f s) -> p f s", f=4), ACT.Copy).then_inc(ht_hi_ready, 1)
                    if n == UP_END(0) + 2:
                        act.wait_ge(placeT_done, rnd + 1)
                        A(place[:, :, :], B[7][:, 0:TC * P].rearrange("p (c t) -> p c t", c=TC), ACT.Copy).then_inc(place_ready, 1)
            load_table(ACT.Sqrt)
            for c in range(TC):
                mean_square(4, c, lambda c, half: (added, rounds * 4 + (2 * c + half + 1)))

        @block.vector
        def _(dve):
            V = nc.vector
            steps = [0]

            def chain(ins):
                steps[0] += 1
                ins.then_inc(dchain, 1)
                dve.wait_ge(dchain, steps[0])

            split_no = [0]

            def split_to(n):
                while split_no[0] <= n:
                    u = split_no[0]
                    split_no[0] += 1
                    dve.wait_ge(hi_ready, u + 1)
                    if u >= U_DENSE:
                        V.tensor_tensor(wlo[:, u - U_DENSE, :], raw_of(u), whi[:, u - U_DENSE, :].bitcast(F32), ALU.subtract).then_inc(lo_ready, 1)
                        continue
                    w = unit_width(u)
                    V.tensor_tensor(dw_lo[:, u % SPLIT_D, 0:w], raw[:, u % RAW, 0:w], dw_hi[:, u % SPLIT_D, 0:w].bitcast(F32),
                                    ALU.subtract).then_inc(lo_ready, 1)

            def resume_splits(unit):
                dve.wait_ge(lo_ready, unit + 1)
                split_no[0] = unit + 1
                split_to(unit + 1)

            def rstd_of(layer, c):
                dve.wait_ge(sq_done, 2 * (TC * layer + c) + 1)
                V.tensor_scalar(mse[:, layer, c:c + 1], ms[:, layer, c, 0:1], EPS, None, ALU.add).then_inc(mse_ready, 1)
                dve.wait_ge(std_ready, TC * layer + c + 1)
                chain(V.reciprocal(rstd[:, layer, c:c + 1], std[:, layer, c:c + 1]))

            def normalise(layer, units=None):
                for c in range(TC):
                    if units is not None:
                        dve.wait_ge(*((c0_done, layer) if c == 0 else (multiplied, units)))
                        for half in range(2):
                            xs = x[:, c, half * 512:(half + 1) * 512]
                            V.tensor_tensor(xs, B[2 * c + half][:, :], xs, ALU.add).then_inc(x_ready, 1)
                    rstd_of(layer, c)
                    for half in range(2):
                        cols = slice(half * 512, (half + 1) * 512)
                        V.tensor_scalar(xn[:, c, cols], x[:, c, cols], rstd[:, layer, c:c + 1], None, ALU.mult).then_inc(xn_ready, 1)

            def low_halves(layer, gain):
                for b in range(2):
                    for c in range(TC):
                        dve.wait_ge(hT_act, TC * KD * layer + 4 * (TC * b + c) + 4)
                        for k in range(4 * b, 4 * b + 4):
                            V.scalar_tensor_tensor(hT_lo[:, k, c * P:(c + 1) * P], turned(layer, c, k), PR(gain)[:, k:k + 1],
                                                   hT_hi[:, k, c * P:(c + 1) * P].bitcast(F32), ALU.mult, ALU.subtract).then_inc(hT_dve, 1)

            def masked_scores(layer, c, scale, mask_of):
                dst, nk = (S0, P) if c == 0 else (S1, SEQ)
                per = 512 // nk
                for b in range(HEADS // per):
                    dve.wait_ge(s_done, 6 * layer + 2 * c + b + 1)
                    last = V.scalar_tensor_tensor(dst[:, b * per:(b + 1) * per, :], B[(0 if c else 4) + b][:, :].rearrange("p (h k) -> p h k", h=per),
                                                  scale, mask_of(c, b * per, (b + 1) * per), ALU.mult, ALU.add)
                last.then_inc(s_read, 1)

            def maxima(layer, c):
                dve.wait_ge(s_read, TC * layer + c + 1)
                chain(V.tensor_reduce(mx[:, c, :], (S0, S1)[c][:, :, :], AX, ALU.max))
                V.tensor_scalar(nmx[:, c, :], mx[:, c, :], -1.0, None, ALU.mult).then_inc(mx_ready, 1)

            def probs_out(layer, b):
                dve.wait_ge(pt_done, 6 * layer + b + 1)
                V.tensor_copy(PT[:, 4 * b:4 * b + 4, :], B[PT_BANK[b]][:, :].rearrange("p (n q) -> p n q", n=4)).then_inc(pt_dve, 1)

            def attention_out(layer, c0, out0):
                split_to(out0 + 1)
                probs_out(layer, 0)
                for c in range(TC):
                    if c:
                        probs_out(layer, 2)
                        probs_out(layer, 4)
                        split_to(out0 + 2)
                    dve.wait_ge(exp_done, 16 * layer + 8 * (c + 1))
                    chain(V.reciprocal(rec[:, c, :], sums[:, c, :]))
                    dve.wait_ge(pv_done, TC * layer + c + 1)
                    V.tensor_tensor(att[:, c, :].rearrange("p (h d) -> p h d", h=HEADS), B[6][:, :].rearrange("p (h d) -> p h d", h=HEADS),
                                    rec[:, c, :].unsqueeze(2).broadcast_to([P, HEADS, VD]), ALU.mult).then_inc(att_ready, 1)
                for b in range(2):
                    dve.wait_ge(attT_hi, 2 * layer + b + 1)
                    rng = slice(c0 + 2 * b, c0 + 2 * b + 2)
                    V.tensor_tensor(mix_lo[:, rng, :], B[4 + b][:, :].rearrange("p (m t) -> p m t", m=2), mix_hi[:, rng, :].bitcast(F32),
                                    ALU.subtract).then_inc(attT_ready, 1)
                split_to(out0 + 3)

            def rotate(buf, x1, x2, cos, sin):
                V.tensor_tensor(buf[0], x1, cos, ALU.mult)
                V.tensor_tensor(buf[1], x2, sin, ALU.mult)
                V.tensor_tensor(buf[2], x2, cos, ALU.mult)
                chain(V.tensor_tensor(buf[3], x1, sin, ALU.mult))
                return buf

            normalise(0)
            split_to(0)
            dve.wait_ge(params_in, 16)
            low_halves(0, "g_mix0")
            split_to(3)
            dve.wait_ge(lsq_done, 4)
            V.tensor_scalar(lmse[:, :, :], lms[:, :, :], EPS, None, ALU.add).then_inc(lmse_ready, 1)
            dve.wait_ge(consts_in, 16)
            cos = C("cos").rearrange("p (c r) -> p c r", c=TC)
            sin = C("sin").rearrange("p (c r) -> p c r", c=TC)
            dve.wait_ge(lat_copied, 2)
            k1, k2 = lat[:, :, QR + KVR:QR + KVR + HR], lat[:, :, QR + KVR + HR:LAT]
            b4 = rotate([ropek[:, n, :, :] for n in range(4)], k1, k2, cos, sin)
            V.tensor_tensor(kr96[:, :, NOPE:NOPE + HR], b4[0], b4[1], ALU.subtract).then_inc(latn_ready, 1)
            V.tensor_tensor(kr96[:, :, NOPE + HR:DQ], b4[2], b4[3], ALU.add).then_inc(latn_ready, 1)
            dve.wait_ge(lstd_ready, 1)
            chain(V.reciprocal(lrstd[:, :, :], lstd[:, :, :]))
            for c in range(TC):
                V.tensor_scalar(latn[:, c, 0:QR], lat[:, c, 0:QR], lrstd[:, 0, c:c + 1], None, ALU.mult)
                last = V.tensor_scalar(latn[:, c, QR:QR + KVR], lat[:, c, QR:QR + KVR], lrstd[:, 1, c:c + 1], None, ALU.mult)
            last.then_inc(latn_ready, 1)
            split_to(4)
            dve.wait_ge(latT_done, 1)
            for m in range(2):
                V.tensor_scalar(latT[:, m, :], B[0][:, m * SEQ:(m + 1) * SEQ], PR("q_norm")[:, m:m + 1], None, ALU.mult).then_inc(latT_ready, 1)
            V.tensor_scalar(latT[:, 2, :], B[1][:, 0:SEQ], PR("kv_norm"), None, ALU.mult).then_inc(latT_ready, 1)
            V.tensor_copy(kT[NOPE:DQ, :, :], B[1][NOPE:DQ, SEQ:2 * SEQ].unsqueeze(1).broadcast_to([ROPE, HEADS, SEQ])).then_inc(kr_ready, 1)
            split_to(5)
            dve.wait_ge(win_ready, POOL_G)
            inv = C("invcnt").rearrange("p (g t) -> p g t", g=POOL_G)
            for g in range(POOL_G):
                win = (win1, win2)[g % 2]
                V.scalar_tensor_tensor(pooled[:, g, :], win[:, g, PAD:], 1.0 / POOL_W[g], apad[:, g, PAD:], ALU.mult, ALU.subtract)
                last = V.tensor_tensor(early[:, g, :], win[:, g, PAD:2 * PAD], inv[:, g, :], ALU.mult)
            chain(last)
            V.tensor_tensor(pooled[:, :, 0:PAD], early[:, :, :], apad[:, :, PAD:2 * PAD], ALU.subtract).then_inc(pooled_ready, 1)
            dve.wait_ge(v_done, 1)
            for c in range(TC):
                V.tensor_copy(vv[:, c, :], B[6 + c][:, :]).then_inc(v_ready, 1)
            dve.wait_ge(q_copied, 4)
            cosh, sinh = (a.unsqueeze(2).broadcast_to([P, TC, HEADS, HR]) for a in (cos, sin))
            q1, q2 = qq[:, :, :, NOPE:NOPE + HR], qq[:, :, :, NOPE + HR:DQ]
            b4 = rotate([ropeq[:, n, :, :].rearrange("p (c h) r -> p c h r", c=TC) for n in range(4)], q1, q2, cosh, sinh)
            V.tensor_tensor(q1, b4[0], b4[1], ALU.subtract).then_inc(q_ready, 1)
            V.tensor_tensor(q2, b4[2], b4[3], ALU.add).then_inc(q_ready, 1)
            for b in (0, 2):
                dve.wait_ge(qT_done, b + 1)
                V.tensor_copy(qT[0:DQ, 2 * b:2 * b + 2, :], B[b][0:DQ, :].rearrange("p (h t) -> p h t", h=2)).then_inc(qT_ready, 1)
            def even_mask(c, h0, h1):
                return C(f"mask{c}").unsqueeze(1).broadcast_to([P, h1 - h0, P * (c + 1)])

            masked_scores(0, 0, DQ ** -0.5, even_mask)
            maxima(0, 0)
            masked_scores(0, 1, DQ ** -0.5, even_mask)
            for g in range(POOL_G):
                dve.wait_ge(pool_hi, 2 * (g // 2) + 2)
                V.scalar_tensor_tensor(mix_lo[:, g, :], B[6 + g // 2][:, (g % 2) * SEQ:(g % 2 + 1) * SEQ], PR("pool_scale")[:, g:g + 1],
                                       mix_hi[:, g, :].bitcast(F32), ALU.mult, ALU.subtract).then_inc(pool_mixed, 1)
            maxima(0, 1)
            attention_out(0, 4, 4)
            normalise(1, U_EVEN)
            low_halves(1, "g_ffn0")
            resume_splits(U_EVEN)
            for step in range(FFS):
                gate = FFN_GATE(step)
                split_to(gate + 2)
                dve.wait_ge(silu_ready, step + 1)
                dve.wait_ge(multiplied, gate + 2)
                if step >= 2:
                    dve.wait_ge(hid_hi_ready, step - 1)
                V.tensor_tensor(hid0[:, step % 2, :], silu0[:, step % 2, :], B[5 + 2 * (step % 2)][:, :], ALU.mult).then_inc(hid_made, 1)
                split_to(gate + 3 if step else gate + 2)
                dve.wait_ge(hid_hi_ready, step + 1)
                V.tensor_tensor(hid_lo[:, step % 2, :], hid0[:, step % 2, :], hid_hi[:, step % 2, :].bitcast(F32), ALU.subtract).then_inc(hid_ready, 1)
            normalise(2, U_ODD0)
            low_halves(2, "g_mix1")
            resume_splits(U_ODD0)
            split_to(U_ODD0 + 2)
            dve.wait_ge(gelu_gv, 2)
            wide = [P, TC * POOL_G, P]
            chain(V.tensor_reduce(gmean[:, :], gv[:, :, :], AX, ALU.add))
            chain(V.tensor_scalar(gmean[:, :], gmean[:, :], -1.0 / P, None, ALU.mult))
            split_to(U_ODD0 + 3)
            chain(V.tensor_tensor(gv[:, :, :], gv[:, :, :], gmean[:, :].unsqueeze(2).broadcast_to(wide), ALU.add))
            chain(V.tensor_tensor(gsq[:, :, :], gv[:, :, :], gv[:, :, :], ALU.mult))
            chain(V.tensor_reduce(gvar[:, :], gsq[:, :, :], AX, ALU.add))
            V.tensor_scalar(gvar[:, :], gvar[:, :], 1.0 / P, EPS, ALU.mult, ALU.add).then_inc(gvar_ready, 1)
            split_to(U_ODD0 + 5)
            dve.wait_ge(gstd_ready, 1)
            chain(V.reciprocal(grs[:, :], gstd[:, :]))
            chain(V.tensor_tensor(gv[:, :, :], gv[:, :, :], grs[:, :].unsqueeze(2).broadcast_to(wide), ALU.mult))
            split_to(U_ODD0 + 6)
            dve.wait_ge(rows_in, 16)
            gv2 = gv[:, :, :].rearrange("p (c g) d -> p c (g d)", c=TC)
            chain(V.tensor_tensor(gv2, gv2, RW("sgu_g").unsqueeze(1).broadcast_to([P, TC, 512]), ALU.mult))
            V.tensor_tensor(gv2, gv2, RW("sgu_nb").unsqueeze(1).broadcast_to([P, TC, 512]), ALU.add).then_inc(vn_ready, 1)
            dve.wait_ge(qz_zeroed, 1)
            for b in range(2):
                dve.wait_ge(multiplied, U_ODD0 + 5 + b)
                src = B[4 + b][:, :].rearrange("p (m t) -> p m t", m=2)
                V.tensor_copy(qT[0:HD, 4 * b:4 * b + 4:2, :], src[0:HD]).then_inc(oq_ready, 1)
                V.tensor_copy(qT[HD:P, 4 * b + 1:4 * b + 4:2, :], src[HD:P]).then_inc(oq_ready, 1)
                split_to(U_ODD0 + 7 + b)
            split_to(U_ODD0 + 9)
            dve.wait_ge(mixed_done, 1)
            sb_row = RW("sgu_b").rearrange("p (g t) -> p g t", g=POOL_G)
            for b in range(2):
                V.tensor_tensor(mixed[:, 2 * b:2 * b + 2, :].rearrange("p g (c t) -> p g c t", c=TC),
                                B[2 + b][:, :].rearrange("p (g c t) -> p g c t", g=2, c=TC),
                                sb_row[:, 2 * b:2 * b + 2, :].unsqueeze(2).broadcast_to([P, 2, TC, P]), ALU.add).then_inc(mixed_read, 1)
            split_to(U_ODD0 + 10)
            dve.wait_ge(bias_ready, 2)

            def biased(c, h0, h1):
                return (bias0, bias1)[c][:, h0:h1, :]

            for c in range(TC):
                masked_scores(1, c, HD ** -0.5, biased)
                maxima(1, c)
            attention_out(1, 0, U_ODD0 + 10)
            normalise(3, U_DENSE)
            for c in range(TC):
                dve.wait_ge(xT_done, 2 * (3 * TC + c + 1))
                for k in range(4, KD):
                    V.tensor_scalar(hT[:, k, c * P:(c + 1) * P], turned(3, c, k), PR("g_ffn1")[:, k:k + 1], None, ALU.mult).then_inc(hT_dve, 1)
            V.memset(slot_of[:, NE + MORE:, :], 0.0)
            V.memset(gate_of[:, 0:1, :], 0.0)
            split_to(U_DENSE)
            for c in range(TC):
                dve.wait_ge(h_hi_ready, c + 1)
                V.tensor_tensor(h_lo[:, c, :], xn[:, c, :], h_hi[:, c, :].bitcast(F32), ALU.subtract).then_inc(h_lo_ready, 1)
            dve.wait_ge(logits_done, 1)
            chain(V.tensor_copy(lg[:, :, :], B[0][:, 0:TC * NE].rearrange("p (c e) -> p c e", c=TC)))
            mine = lg[:, :, :].unsqueeze(3).broadcast_to([P, TC, NE, NE])
            other = lg[:, :, :].unsqueeze(2).broadcast_to([P, TC, NE, NE])
            gt4 = gt[:, :, :].rearrange("p (c e) f -> p c e f", c=TC)
            eq4 = eq[:, :, :].rearrange("p (c e) f -> p c e f", c=TC)
            low = C("low").rearrange("p (e f) -> p e f", e=NE)
            V.tensor_tensor(gt4, other, mine, ALU.is_gt)
            chain(V.tensor_tensor(eq4, other, mine, ALU.is_equal))
            chain(V.tensor_tensor(eq4, eq4, low.unsqueeze(1).broadcast_to([P, TC, NE, NE]), ALU.mult))
            chain(V.tensor_tensor(gt[:, :, :], gt[:, :, :], eq[:, :, :], ALU.add))
            chain(V.tensor_reduce(rank[:, :, :], gt4, AX, ALU.add))
            V.tensor_scalar(chosen[:, :, :], rank[:, :, :], 1.5, None, ALU.is_lt).then_inc(chosen_ready, 1)
            chain(V.tensor_scalar(first[:, :, :], rank[:, :, :], 0.5, None, ALU.is_lt))
            V.tensor_tensor(second[:, :, :], chosen[:, :, :], first[:, :, :], ALU.subtract)
            chain(V.tensor_tensor(tmp8[:, :, :], first[:, :, :], lg[:, :, :], ALU.mult))
            chain(V.tensor_reduce(v1[:, :], tmp8[:, :, :], AX, ALU.add))
            chain(V.tensor_tensor(tmp8[:, :, :], second[:, :, :], lg[:, :, :], ALU.mult))
            chain(V.tensor_reduce(v2[:, :], tmp8[:, :, :], AX, ALU.add))
            V.tensor_tensor(dv[:, :], v2[:, :], v1[:, :], ALU.subtract).then_inc(dv_ready, 1)
            dve.wait_ge(pos_done, 1)
            V.scalar_tensor_tensor(slot_of[:, 0:NE, :].rearrange("p r c -> p c r"), B[1][:, 0:TC * NE].rearrange("p (c e) -> p c e", c=TC),
                                   1.0, chosen[:, :, :], ALU.add, ALU.mult).then_inc(slots_ready, 1)

            def picks(rnd):
                for c in range(TC):
                    col = slot_of[:, bass.ds(rnd, 1), c]
                    V.tensor_scalar(pick[:, c, :], C("slot"), col, None, ALU.is_equal).then_inc(pick_ready, 1)
                    V.tensor_scalar(pickr[:, c, :], C("slot"), col, None, ALU.is_equal).then_inc(pick_ready, 1)

            def packed_out(rnd):
                for b in range(2):
                    dve.wait_ge(xe_hi_ready, rnd * 2 + (b + 1))
                    V.tensor_tensor(xe_lo[:, 4 * b:4 * b + 4, :], B[4 + b][:, :].rearrange("p (k s) -> p k s", k=4),
                                    xe_hi[:, 4 * b:4 * b + 4, :].bitcast(F32), ALU.subtract).then_inc(xe_ready, 1)

            def result_out(rnd):
                for half in range(2):
                    dve.wait_ge(y_hi_ready, (rnd - 1) * 2 + (half + 1))
                    cols = slice(half * 512, (half + 1) * 512)
                    V.tensor_tensor(y_lo[:, cols], B[half][:, :], y_hi[:, cols].bitcast(F32), ALU.subtract).then_inc(y_ready, 1)

            def add_back(rnd):
                for c in range(TC):
                    for half in range(2):
                        dve.wait_ge(scattered, rnd * 4 + (2 * c + half + 1))
                        xs = x[:, c, half * 512:(half + 1) * 512]
                        V.scalar_tensor_tensor(xs, B[4 + 2 * c + half][:, :], gate_of[:, bass.ds(rnd, 1), c], xs, ALU.mult, ALU.add).then_inc(added, 1)

            dve.wait_ge(slots_ready, 1)
            picks(0)
            chain(V.tensor_scalar(over[:, :], B[1][:, 2 * NE:3 * NE], P + 0.5, None, ALU.is_gt))
            chain(V.tensor_reduce(info_f[:, 0:1], over[:, :], AX, ALU.add))
            V.tensor_scalar(info[:, 0:1], info_f[:, 0:1], float(NE), None, ALU.add).then_inc(route_ready, 1)
            resume_splits(U_DENSE + 1)
            dve.wait_ge(ev_ready, 1)
            chain(V.tensor_scalar(w1[:, :], ev[:, :], 1.0, None, ALU.add))
            chain(V.reciprocal(w1[:, :], w1[:, :]))
            chain(V.tensor_tensor(w2[:, :], ev[:, :], w1[:, :], ALU.mult))
            packed_out(0)
            V.tensor_tensor(first[:, :, :], first[:, :, :], w1[:, :].unsqueeze(2).broadcast_to([P, TC, NE]), ALU.mult)
            chain(V.tensor_tensor(second[:, :, :], second[:, :, :], w2[:, :].unsqueeze(2).broadcast_to([P, TC, NE]), ALU.mult))
            V.tensor_tensor(gate_of[:, 1:NE + 1, :].rearrange("p r c -> p c r"), first[:, :, :], second[:, :, :], ALU.add)
            chain(V.tensor_tensor(eq[:, 0:NE, :], low, over[:, :].unsqueeze(1).broadcast_to([P, NE, NE]), ALU.mult))
            chain(V.tensor_reduce(kx[:, :], eq[:, 0:NE, :], AX, ALU.add))
            for j in range(MORE):
                last = V.scalar_tensor_tensor(mj[:, j, :], kx[:, :], float(j), over[:, :], ALU.is_equal, ALU.mult)
            last.then_inc(tables_ready, 1)
            dve.wait_ge(route_ready, 1)
            rounds = dve.value_load(info[0:1, 0:1], min_val=NE, max_val=ROUNDS)
            with dve.Fori(0, rounds) as rnd:
                for n in range(SPLIT, U_EXP + SPLIT):
                    dve.wait_ge(hi_ready, rnd * U_EXP + (U_DENSE + n + 1))
                    V.tensor_tensor(wlo[:, n % SPLIT, :], raw_of(U_DENSE + n), whi[:, n % SPLIT, :].bitcast(F32), ALU.subtract).then_inc(lo_ready, 1)
                    if n == U_EXP + 1:
                        result_out(rnd + 1)
                    for j in range(JB):
                        if n == UP_END(j) + 2:
                            dve.wait_ge(sg_ready_m, rnd * JB + (j + 1))
                            dve.wait_ge(multiplied, rnd * U_EXP + (U_DENSE + UP_END(j) + 1))
                            V.tensor_tensor(hid[:, j % 2, :], sg[:, j % 2, :], B[3 + 2 * (j % 2)][:, :], ALU.mult).then_inc(hid_ready_m, 1)
                        if n == HT_AT(j) and j == JB - 1:
                            packed_out(rnd + 1)
                        if n == HT_AT(j):
                            dve.wait_ge(ht_hi_ready, rnd * JB + (j + 1))
                            V.tensor_tensor(ht_lo[:, j % 2, :, :], B[6][:, :].rearrange("p (f s) -> p f s", f=4),
                                            ht_hi[:, j % 2, :, :].bitcast(F32), ALU.subtract).then_inc(ht_ready, 1)
                    if n == SPLIT + 1:
                        add_back(rnd)
                    if n == UP_END(JB - 1):
                        dve.wait_ge(placeT_done, rnd + 1)
                        dve.wait_ge(later_ready, 1)
                        picks(rnd + 1)
            add_back(rounds)
            dve.wait_ge(g_final_in, 16)
            for c in range(TC):
                rstd_of(4, c)
                for half in range(2):
                    cols = slice(half * 512, (half + 1) * 512)
                    V.scalar_tensor_tensor(xn[:, c, cols], x[:, c, cols], rstd[:, 4, c:c + 1], g_final[:, cols], ALU.mult, ALU.mult).then_inc(final_ready, 1)


def kernel(**inputs):
    from concourse import bacc
    from concourse.bass_utils import run_bass_kernel_spmd

    a = {k: np.asarray(v) for k, v in inputs.items()}

    def column(v):
        return v.reshape(-1, P).T

    params = np.concatenate([
        column(a["ev_norm_mix"][0]), column(a["ev_norm_ffn"][0]), column(a["od_norm_mix"][0]), column(a["od_norm_ffn"][0]),
        a["ev_pool_scale"][0].T, column(a["ev_q_norm"][0]), column(a["ev_kv_norm"][0]),
        a["od_router"][0].reshape(KD, P, NE).transpose(1, 0, 2).reshape(P, -1),
        a["ev_pool_w"][0].transpose(1, 0, 2).reshape(P, -1),
        a["od_sgu_w"][0].transpose(2, 0, 1).reshape(P, -1)], axis=1)
    rows = np.concatenate([a["od_sgu_b"][0].reshape(-1), a["od_sgu_norm_g"][0].reshape(-1), a["od_sgu_norm_b"][0].reshape(-1)])
    offset = np.clip(np.arange(SEQ)[:, None] - np.arange(SEQ)[None, :], -REL, REL) + REL
    bias = a["od_rel_bias"][0][:, offset].transpose(1, 0, 2)
    arrays = {"x": a["x"], "consts": constants(), "params": params, "rows": rows, "g_ffn1": a["od_norm_ffn"][0], "g_final": a["final_norm"], "bias0": bias[0:P, :, 0:P], "bias1": bias[P:SEQ]}
    for name in ("ev_w_in", "ev_w_q_up", "ev_w_kv_up", "ev_w_out", "ev_ffn_w_gate", "ev_ffn_w_up", "ev_ffn_w_down", "od_w_in", "od_w_out",
                 "od_moe_w_gate", "od_moe_w_up", "od_moe_w_down"):
        arrays[name] = a[name][0]
    nc = bacc.Bacc("TRN2", target_bir_lowering=False, num_devices=1)
    feeds, t = {}, {}
    for name, v in arrays.items():
        v = np.ascontiguousarray(v)
        feeds[f"in_{name}"] = v
        t[name] = nc.dram_tensor(f"in_{name}", v.shape, mybir.dt.from_np(v.dtype), kind="ExternalInput").ap()
    t["out"] = nc.dram_tensor("out_0", (1, SEQ, D), F32, kind="ExternalOutput").ap()
    build(nc, t)
    r = run_bass_kernel_spmd(nc, [feeds], core_ids=[0])
    return r.results[0]["out_0"]
```
